# Optimizing a Trainium2 kernel written in Bass

```python
import jax, jax.numpy as jnp
from jax import lax
import numpy as np

D_MODEL = 1024
BATCH = 1
SEQ = 512
DEPTH = 1

MIX_WIDTH = D_MODEL
CONV_WIDTH = MIX_WIDTH // 2
CONV_GROUPS = 8
CONV_K = 3
HGRN_WIDTH = MIX_WIDTH - CONV_WIDTH
HGRN_HEAD_DIM = 128
HGRN_HEADS = HGRN_WIDTH // HGRN_HEAD_DIM
CHUNK = 64
IN_COLS = 3 * CONV_WIDTH + 4 * HGRN_WIDTH
N_MEM = 256
MEM_HEADS = 4
MEM_HEAD_DIM = D_MODEL // MEM_HEADS
PEER_HEADS = 8
PEER_N_KEYS = 128
PEER_N_EXPERTS = PEER_N_KEYS * PEER_N_KEYS
PEER_DK = 128
PEER_TOPK = 16
PEER_BLOCK = 128
EPS = 1e-6

kernel_name = "hymba_conv_hgrn2_memxattn_peer"

def rmsnorm(x, w):
    xf = x.astype(jnp.float32)
    y = xf * lax.rsqrt(jnp.mean(xf * xf, axis=-1, keepdims=True) + EPS)
    return (y * w.astype(jnp.float32)).astype(x.dtype)

def short_conv_mixer(b_gate, c_gate, v, conv_w):
    T = v.shape[1]
    u = c_gate * v
    up = jnp.pad(u, ((0, 0), (CONV_K - 1, 0), (0, 0)))
    y = up[:, 0:T] * conv_w[0]
    for j in range(1, CONV_K):
        y = y + up[:, j:j + T] * conv_w[j]
    return b_gate * y

def hgrn2_mixer(q, f, i, g, lb, norm_w):
    B, T, _ = q.shape
    H, Dh, C = HGRN_HEADS, HGRN_HEAD_DIM, CHUNK
    N = T // C
    f32 = jnp.float32
    qa = jax.nn.silu(q.astype(f32))
    fg = lb.astype(f32) + (1.0 - lb.astype(f32)) * jax.nn.sigmoid(f.astype(f32))
    k = 1.0 - fg
    logf = jnp.log(fg)

    def heads(a):
        return a.reshape(B, N, C, H, Dh).transpose(0, 3, 1, 2, 4)

    qh, kh, lh, vh = heads(qa), heads(k), heads(logf), heads(i.astype(f32))
    G = jnp.cumsum(lh, axis=3)
    G_last = G[:, :, :, -1:]
    q_dec = qh * jnp.exp(G)
    k_inv = kh * jnp.exp(-G)
    k_to_end = kh * jnp.exp(G_last - G)
    causal = jnp.tril(jnp.ones((C, C), dtype=bool))
    A = jnp.where(causal, jnp.einsum('bhnck,bhnsk->bhncs', q_dec, k_inv), 0.0)
    o_intra = jnp.einsum('bhncs,bhnsv->bhncv', A, vh)
    U = jnp.einsum('bhnck,bhncv->bhnkv', k_to_end, vh)
    decay = jnp.exp(G_last[:, :, :, 0])

    def step(S, xs):
        d_n, U_n = xs
        return d_n[..., None] * S + U_n, S

    S0 = jnp.zeros((B, H, Dh, Dh), f32)
    _, S_start = lax.scan(step, S0, (jnp.moveaxis(decay, 2, 0), jnp.moveaxis(U, 2, 0)))
    S_start = jnp.moveaxis(S_start, 0, 2)
    o = o_intra + jnp.einsum('bhnck,bhnkv->bhncv', q_dec, S_start)
    o = o.transpose(0, 2, 3, 1, 4).reshape(B, T, H, Dh)
    o = o * lax.rsqrt(jnp.mean(o * o, axis=-1, keepdims=True) + EPS)
    o = o.reshape(B, T, H * Dh) * norm_w.astype(f32) * jax.nn.silu(g.astype(f32))
    return o.astype(q.dtype)

def memory_cross_attention(h, mem_n, wq, wkv, wo):
    B, T, _ = h.shape
    M = mem_n.shape[1]
    q = (h @ wq).reshape(B, T, MEM_HEADS, MEM_HEAD_DIM)
    kv = mem_n @ wkv
    k = kv[..., :D_MODEL].reshape(B, M, MEM_HEADS, MEM_HEAD_DIM)
    v = kv[..., D_MODEL:].reshape(B, M, MEM_HEADS, MEM_HEAD_DIM)
    s = jnp.einsum('bthd,bmhd->bhtm', q, k).astype(jnp.float32) * (MEM_HEAD_DIM ** -0.5)
    p = jax.nn.softmax(s, axis=-1).astype(v.dtype)
    o = jnp.einsum('bhtm,bmhd->bthd', p, v).reshape(B, T, D_MODEL)
    return o @ wo

def peer_ffn(h, w_query, sub_keys, expert_down, expert_up):
    B, T, D = h.shape
    Ntok = B * T
    K = PEER_TOPK
    tokens = h.reshape(Ntok, D)
    q = (tokens @ w_query).reshape(Ntok, PEER_HEADS, 2, PEER_DK)
    s = jnp.einsum('nhpd,hpkd->nhpk', q, sub_keys).astype(jnp.float32)
    s_top, i_top = lax.top_k(s, K)
    cand = (s_top[:, :, 0, :, None] + s_top[:, :, 1, None, :]).reshape(Ntok, PEER_HEADS, K * K)
    cand_idx = (i_top[:, :, 0, :, None] * PEER_N_KEYS + i_top[:, :, 1, None, :]).reshape(Ntok, PEER_HEADS, K * K)
    best, pos = lax.top_k(cand, K)
    expert_idx = jnp.take_along_axis(cand_idx, pos, axis=-1)
    gate = jax.nn.softmax(best, axis=-1)
    nb = Ntok // PEER_BLOCK

    def block(args):
        xb, idx, gb = args
        u = jnp.take(expert_down, idx, axis=0)
        a = jax.nn.gelu(jnp.einsum('nd,nhkd->nhk', xb, u).astype(jnp.float32), approximate=False)
        w = (gb * a).astype(xb.dtype)
        v = jnp.take(expert_up, idx, axis=0)
        return jnp.einsum('nhk,nhkd->nd', w, v)

    out = lax.map(block, (tokens.reshape(nb, PEER_BLOCK, D),
                          expert_idx.reshape(nb, PEER_BLOCK, PEER_HEADS, K),
                          gate.reshape(nb, PEER_BLOCK, PEER_HEADS, K)))
    return out.reshape(B, T, D)

def setup_inputs(seed: int = 0) -> dict:
    key = jax.random.key(seed)
    ks = jax.random.split(key, 24)
    f32 = jnp.float32
    L, D = DEPTH, D_MODEL

    def nrm(k, shape, scale):
        return jax.random.normal(k, shape, f32) * scale

    def gain(k, shape):
        return 1.0 + 0.02 * jax.random.normal(k, shape, f32)

    return {
        "x": jax.random.normal(ks[0], (BATCH, SEQ, D), f32),
        "mem": jax.random.normal(ks[1], (BATCH, N_MEM, D), f32),
        "mix_norm_w": gain(ks[2], (L, D)),
        "w_in": nrm(ks[3], (L, D, IN_COLS), D ** -0.5),
        "conv_w": nrm(ks[4], (L, CONV_K, CONV_WIDTH), CONV_K ** -0.5),
        "conv_norm_w": gain(ks[5], (L, CONV_WIDTH)),
        "hgrn_lb_logits": 0.1 * jax.random.normal(ks[6], (L + 1, HGRN_WIDTH), f32),
        "hgrn_norm_w": gain(ks[7], (L, HGRN_WIDTH)),
        "w_out": nrm(ks[8], (L, MIX_WIDTH, D), MIX_WIDTH ** -0.5),
        "xattn_norm_w": gain(ks[9], (L, D)),
        "mem_norm_w": gain(ks[10], (L, D)),
        "wq_mem": nrm(ks[11], (L, D, D), D ** -0.5),
        "wkv_mem": nrm(ks[12], (L, D, 2 * D), D ** -0.5),
        "wo_mem": nrm(ks[13], (L, D, D), D ** -0.5),
        "ffn_norm_w": gain(ks[14], (L, D)),
        "peer_w_query": nrm(ks[15], (L, D, PEER_HEADS * 2 * PEER_DK), D ** -0.5),
        "peer_sub_keys": nrm(ks[16], (L, PEER_HEADS, 2, PEER_N_KEYS, PEER_DK), PEER_DK ** -0.5),
        "peer_down": nrm(ks[17], (L, PEER_N_EXPERTS, D), D ** -0.5),
        "peer_up": nrm(ks[18], (L, PEER_N_EXPERTS, D), 0.5),
        "final_norm_w": gain(ks[19], (D,)),
    }

def reference(x, mem, mix_norm_w, w_in, conv_w, conv_norm_w, hgrn_lb_logits, hgrn_norm_w, w_out,
              xattn_norm_w, mem_norm_w, wq_mem, wkv_mem, wo_mem, ffn_norm_w,
              peer_w_query, peer_sub_keys, peer_down, peer_up, final_norm_w):
    lb_all = jnp.cumsum(jax.nn.softmax(hgrn_lb_logits.astype(jnp.float32), axis=0), axis=0)
    cw, hw = CONV_WIDTH, HGRN_WIDTH
    for l in range(DEPTH):
        h = rmsnorm(x, mix_norm_w[l])
        proj = h @ w_in[l]
        b_gate = proj[..., 0:cw]
        c_gate = proj[..., cw:2 * cw]
        v_conv = proj[..., 2 * cw:3 * cw]
        o0 = 3 * cw
        q_h = proj[..., o0:o0 + hw]
        f_h = proj[..., o0 + hw:o0 + 2 * hw]
        i_h = proj[..., o0 + 2 * hw:o0 + 3 * hw]
        g_h = proj[..., o0 + 3 * hw:o0 + 4 * hw]
        y_conv = rmsnorm(short_conv_mixer(b_gate, c_gate, v_conv, conv_w[l]), conv_norm_w[l])
        y_hgrn = hgrn2_mixer(q_h, f_h, i_h, g_h, lb_all[l], hgrn_norm_w[l])
        x = x + jnp.concatenate([y_conv, y_hgrn], axis=-1) @ w_out[l]
        h = rmsnorm(x, xattn_norm_w[l])
        mem_n = rmsnorm(mem, mem_norm_w[l])
        x = x + memory_cross_attention(h, mem_n, wq_mem[l], wkv_mem[l], wo_mem[l])
        h = rmsnorm(x, ffn_norm_w[l])
        x = x + peer_ffn(h, peer_w_query[l], peer_sub_keys[l], peer_down[l], peer_up[l])
    return rmsnorm(x, final_norm_w)


_drawn_inputs = setup_inputs


def setup_inputs(seed=0):
    import zlib

    import numpy as np

    out = dict(_drawn_inputs(seed))
    spreads = {}
    factors = {'hgrn_lb_logits': 4.178,
     'hgrn_norm_w': 3.102,
     'xattn_norm_w': 6.272,
     'mem_norm_w': 5.1,
     'final_norm_w': 8.062,
     'ffn_norm_w': 7.712}
    for name, (base, spread) in spreads.items():
        noise = np.random.default_rng([zlib.crc32(name.encode()), seed]).standard_normal(out[name].shape)
        drawn = base * np.exp(spread * noise) if base else spread * noise
        out[name] = __import__('jax').numpy.asarray(drawn.astype(out[name].dtype))
    for name, factor in factors.items():
        out[name] = (out[name] * factor).astype(out[name].dtype)
    return out
```

```python
from contextlib import ExitStack

import concourse.bass as bass
from concourse import mybir

F32 = mybir.dt.float32
U32 = mybir.dt.uint32
ALU = mybir.AluOpType
ACT = mybir.ActivationFunctionType
AX_X = mybir.AxisListType.X

P = 128
D = 1024
KC = D // P
SEQ = 512
NT = SEQ // P
NM = 256
MT = NM // P
CW = 512
CC = CW // P
HH = 4
CH = 64
NCH = SEQ // CH
MH = 4
DH = D // MH
PH = 8
NK = 128
TK = 16
NEG = -3.0e38
EPS = 1e-6

RING = 4
BLOCKS = 84
GT = 4
GROUPS = NK // GT
TB = 8

V_MIX, V_CONV, V_HGRN, V_LB0, V_LB1, V_ATT, V_MEM, V_FFN, V_CW = 0, 8, 12, 16, 20, 24, 32, 40, 48
NV = V_CW + 3 * CC


def build(nc, x_in, mem_in, vecs_in, final_in, front_w, keys_in, down_in, up_in, out, gate_dram):
    ctx = ExitStack()
    with ctx:
        def sem(name):
            return ctx.enter_context(nc.semaphore(name))

        KB = 256
        arena = ctx.enter_context(nc.sbuf_tensor("arena", [P, 206 * KB], F32))
        psum = ctx.enter_context(nc.psum_tensor("psum", [P, 8, 512], F32))

        def at(kb, n, *dims):
            a = arena[:, int(kb * KB):int(kb * KB) + n]
            if len(dims) == 2:
                return a.rearrange("p (a b) -> p a b", a=dims[0])
            if len(dims) == 3:
                return a.rearrange("p (a b c) -> p a b c", a=dims[0], b=dims[1])
            return a

        x = at(0, NT * D, NT, D)
        vec = at(16, NV)
        ident = at(16.5, P)
        ones = at(17, P)
        iota = at(17.5, P)
        causal = at(18, P)
        fin_w = at(18.5, D)
        ss = at(22.5, 16)
        ms = at(22.5625, 16)
        rt = at(22.625, 16)
        rs = at(22.6875, 16)
        lbm = at(22.75, 32)
        lb, oml = lbm[:, 20:24], lbm[:, 24:28]
        decay = at(23, HH * NCH, HH, NCH)
        mx, nmx, den, rden = (at(23.25 + 0.0625 * j, 16) for j in range(4))
        junk = at(23.5, D)
        ring = at(28, RING * D, RING, D)
        hn = at(44, NT * D, NT, D)
        hT = at(60, KC * SEQ, KC, SEQ)
        proj = at(76, 24 * SEQ, 24, SEQ)
        pB, pC, pV, pQ, pF, pG = (proj[:, 4 * j:4 * j + 4, :] for j in range(6))
        iN = at(124, NT * CW, NT, CW)
        memT = at(132, KC * NM, KC, NM)
        KT = at(140, KC * NM, KC, NM)
        Vm = at(148, MT * D, MT, D)
        mem = at(156, MT * D, MT, D)
        fgate, qsil, gsil = (at(164 + 8 * j, HH * SEQ, HH, SEQ) for j in range(3))
        kk = at(188, HH * SEQ, HH, SEQ)
        G = at(196, HH * SEQ, HH, SEQ)
        logf = at(44, HH * SEQ, HH, SEQ)
        expG = at(52, HH * SEQ, HH, SEQ)
        expN = at(60, HH * SEQ, HH, SEQ)
        expD = at(68, HH * SEQ, HH, SEQ)
        aT = pC
        keN = pV
        S = at(44, HH * NCH * P, HH, NCH, P)
        sq = at(60, HH * SEQ, HH, SEQ)
        rinv = at(68, HH * SEQ, HH, SEQ)
        yT = at(188, KC * SEQ, KC, SEQ)
        csq = at(156, CC * SEQ, CC, SEQ)
        reset = at(204, SEQ)
        qT = at(76, KC * SEQ, KC, SEQ)
        prob = at(92, 2 * NT * NM, 2, NT, NM)
        pT = at(100, 2 * MT * SEQ, 2, MT, SEQ)
        aoT = at(108, KC * SEQ, KC, SEQ)
        qpT = at(76, 16 * SEQ, 16, SEQ)
        score = at(116, NT * 16 * NK, NT, 16 * NK)
        cand = at(156, PH * TK * TK, PH, TK * TK)
        onehot = at(164, PH * TK * TK, PH, TK * TK)
        picked = at(172, PH * TK * TK, PH, TK * TK)
        keysT = at(180, 16 * NK, 16, NK)
        top = at(188, 16 * TK, 16, TK)
        topi = at(189, 16 * TK, 16, TK)
        topf = at(190, 16 * TK, 16, TK)
        best = at(191, PH * TK, PH, TK)
        pos = at(191.5, PH * TK, PH, TK)
        posd = at(192, PH * TK, PH, TK)
        posf = at(192.5, 2 * PH * TK, 2, PH, TK)
        ebest = at(193.5, PH * TK, PH, TK)
        hk = at(194, 3 * P, 3, P)
        esum = at(195.5, 16)
        hkT = at(44, 3 * SEQ, 3, SEQ)
        hot = at(28, 2 * 2 * TB * P, 2, 2, TB * P)
        stage = at(76, 2 * P * P, 2, P, P)
        down = at(76, 2 * GT * D, 2, GT, D)
        up = at(108, 2 * GT * D, 2, GT, D)
        gates = at(140, 2 * GT * SEQ, 2, GT, SEQ)
        wgt = at(156, 2 * GT * SEQ, 2, GT, SEQ)
        hid = at(172, 2 * SEQ, 2, SEQ)

        ld_x, ld_mem, ld_vec, ld_fin, ld_keys = (sem(n) for n in ("ld_x", "ld_mem", "ld_vec", "ld_fin", "ld_keys"))
        wt = [sem(f"weight_slot{s}") for s in range(RING)]
        block_used = sem("block_used")
        consts = sem("consts")
        class Norm:
            def __init__(self, name, src, dst, hT, tiles, gain):
                self.src, self.dst, self.hT, self.tiles, self.gain = src, dst, hT, tiles, gain
                self.sumsq, self.mean, self.root, self.h, self.tr, self.ready = (
                    sem(f"{name}_{s}") for s in ("sumsq", "mean", "root", "h", "transposed", "ready"))

        mixn = Norm("mix", x, hn, hT, NT, V_MIX)
        memn = Norm("mem", mem, mem, memT, MT, V_MEM)
        attn = Norm("att", x, hn, hT, NT, V_ATT)
        ffnn = Norm("ffn", x, hn, hT, NT, V_FFN)
        bank_free = sem("bank_free")
        i_out, k_out, v_out = sem("i_out"), sem("k_out"), sem("v_out")
        i_done, v_done = sem("i_done"), sem("v_done")
        lb_diff, lb_exp = sem("lb_diff"), sem("lb_exp")
        exp_fqg, fg_ready, logf_ready, G_ready, expG_ready, qk_ready = (
            sem(n) for n in ("exp_fqg", "fg_ready", "logf_ready", "G_ready", "expG_ready", "qk_ready"))
        conv_sq, conv_sum, conv_root, conv_y = (sem(n) for n in ("conv_sq", "conv_sum", "conv_root", "conv_y"))
        ke_tr, ke_out, a_done, a_ready = (sem(n) for n in ("ke_tr", "ke_out", "a_done", "a_ready"))
        u_done, u_used, s_ready, o_done, o_sq, o_sum, o_root, y_ready = (
            sem(n) for n in ("u_done", "u_used", "s_ready", "o_done", "o_sq", "o_sum", "o_root", "y_ready"))
        mix_done, x_mixed = sem("mix_done"), sem("x_mixed")
        q_out, sc_done, sc_max, sc_exp, p_ready, p_tr, pT_out, ao_done, ao_out = (
            sem(n) for n in ("q_out", "sc_done", "sc_max", "sc_exp", "p_ready", "p_tr", "pT_out", "ao_done", "ao_out"))
        att_done, x_att = sem("att_done"), sem("x_att")
        qp_out, pk_done, pk_out = sem("qp_out"), sem("pk_done"), sem("pk_out")
        best_ready, e_ready, hk_ready, hk_tr, hkT_out = (
            sem(n) for n in ("best_ready", "e_ready", "hk_ready", "hk_tr", "hkT_out"))
        hot_ready, gate_done, gate_out = (sem(n) for n in ("hot_ready", "gate_done", "gate_out"))
        stored = [sem(f"gates_stored{s}") for s in range(2)]
        ld_down = [sem(f"ld_down{s}") for s in range(2)]
        ld_up = [sem(f"ld_up{s}") for s in range(2)]
        ld_gate = [sem(f"ld_gate{s}") for s in range(2)]
        hid_done, gelu_out, w_ready, up_done, x_added = (
            sem(n) for n in ("hid_done", "gelu_out", "w_ready", "up_done", "x_added"))
        fin_sq, fin_mean, fin_root, fin_y, out_stored = (
            sem(n) for n in ("fin_sq", "fin_mean", "fin_root", "fin_y", "out_stored"))
        dve_step, act_step, pool_step = sem("dve_step"), sem("act_step"), sem("pool_step")

        class Steps:
            def __init__(self, eng, own):
                self.eng, self.own, self.n = eng, own, 0

            def __call__(self, ins):
                ins.then_inc(self.own, 1)
                self.n += 1
                self.eng.wait_ge(self.own, self.n)

        block = ctx.enter_context(nc.Block())

        @block.sync
        def _(sp):
            for s in range(RING):
                sp.dma_start(ring[:, s, :], front_w[s]).then_inc(wt[s], 16)
            with sp.Fori(1, BLOCKS // RING) as r:
                for s in range(RING):
                    b = sp.snap(r * RING + s)
                    sp.wait_ge(block_used, r * RING + (s + 1 - RING))
                    sp.dma_start(ring[:, s, :], front_w[bass.ds(b, 1)].rearrange("b p n -> (b p) n"))\
                        .then_inc(wt[s], 16)
            for s in range(2):
                sp.wait_ge(stored[s], 16 * NT // 2)

            def load_down(g, s):
                sp.dma_start(down[:, s], down_in[bass.ds(g, 1)].rearrange("g t p n -> p (g t) n")).then_inc(ld_down[s], 16)

            def load_gates(g, s):
                sp.dma_start(gates[:, s], gate_dram[:, bass.ds(g * GT, GT), :]).then_inc(ld_gate[s], 16)

            def load_up(g, s):
                sp.dma_start(up[:, s], up_in[bass.ds(g, 1)].rearrange("g t p n -> p (g t) n")).then_inc(ld_up[s], 16)

            for s in range(2):
                load_down(s, s)
                load_gates(s, s)
                load_up(s, s)
            with sp.Fori(1, GROUPS // 2) as r:
                for s in range(2):
                    sp.wait_ge(hid_done, r * (2 * GT) + (s - 1) * GT)
                    load_down(r * 2 + s, s)
                    sp.wait_ge(w_ready, r * (2 * GT) + ((s - 1) * GT + 2))
                    load_gates(r * 2 + s, s)
                    sp.wait_ge(up_done, r * 16 + (s - 1) * 8)
                    load_up(r * 2 + s, s)
            for t in range(NT):
                sp.wait_ge(fin_y, t + 1)
                sp.dma_start(out[t * P:(t + 1) * P, :], hn[:, t, :]).then_inc(out_stored, 16)
            sp.wait_ge(out_stored, 16 * NT)

        @block.gpsimd
        def _(pool):
            step = Steps(pool, pool_step)
            nc.gpsimd.memset(ones, 1.0).then_inc(consts, 1)
            step(nc.gpsimd.memset(ident, 0.0))
            nc.gpsimd.affine_select(out=ident, in_=ident, compare_op=ALU.not_equal, fill=1.0, base=0,
                                    pattern=[[-1, P]], channel_multiplier=1).then_inc(consts, 1)
            step(nc.gpsimd.memset(causal, 1.0))
            step(nc.gpsimd.affine_select(out=causal, in_=causal, compare_op=ALU.is_ge, fill=0.0, base=0,
                                         pattern=[[1, P]], channel_multiplier=-1))
            nc.gpsimd.affine_select(out=causal[:, CH:P], in_=causal[:, CH:P], compare_op=ALU.is_ge, fill=0.0,
                                    base=-CH, pattern=[[0, P - CH]], channel_multiplier=1).then_inc(consts, 1)
            nc.gpsimd.iota(iota, pattern=[[1, P]], base=0, channel_multiplier=0,
                           allow_small_or_imprecise_dtypes=True).then_inc(consts, 1)
            step(nc.gpsimd.memset(reset, 1.0))
            nc.gpsimd.memset(reset.rearrange("p (c t) -> p c t", t=CH)[:, :, 0:1], 0.0).then_inc(consts, 1)

        @block.scalar
        def _(act):
            act.dma_start(x, x_in.rearrange("(t p) d -> p t d", p=P)).then_inc(ld_x, 16)
            act.dma_start(vec, vecs_in).then_inc(ld_vec, 16)
            act.dma_start(mem, mem_in.rearrange("(t p) d -> p t d", p=P)).then_inc(ld_mem, 16)
            act.dma_start(fin_w, final_in.to_broadcast([P, D])).then_inc(ld_fin, 16)
            act.sem_inc(bank_free, 4)
            act.sem_inc(gelu_out, 2)

            def norm(u, col):
                for t in range(u.tiles):
                    nc.scalar.activation(junk, u.src[:, t, :], ACT.Square, accum_out=ss[:, col + t:col + t + 1])\
                        .then_inc(u.sumsq, 1)
                    act.wait_ge(u.sumsq, t + 1)
                act.wait_ge(u.mean, 1)
                nc.scalar.activation(rt[:, col:col + u.tiles], ms[:, col:col + u.tiles], ACT.Sqrt).then_inc(u.root, 1)

            act.wait_ge(ld_x, 16)
            norm(mixn, 0)
            act.wait_ge(ld_mem, 16)
            norm(memn, 4)
            act.wait_ge(lb_diff, 1)
            nc.scalar.activation(lbm[:, 4:12], lbm[:, 4:12], ACT.Exp).then_inc(lb_exp, 1)
            with act.Fori(0, 6) as r:
                for s in range(4):
                    act.wait_ge(block_used, r * 4 + (s + 1))
                    nc.scalar.activation(proj[:, bass.ds(r * 4 + s, 1), :], psum[:, s:s + 1, :], ACT.Copy)\
                        .then_inc(bank_free, 1)
            act.wait_ge(bank_free, 28)
            for a, b in ((fgate, pF), (qsil, pQ), (gsil, pG)):
                nc.scalar.activation(a, b, ACT.Exp, scale=-1.0).then_inc(exp_fqg, 1)
            act.wait_ge(i_done, 1)
            for t in range(NT):
                nc.scalar.activation(iN[:, t, :], psum[:, 4 + t, :], ACT.Copy).then_inc(i_out, 1)
            act.wait_ge(fg_ready, 1)
            nc.scalar.activation(logf, fgate, ACT.Ln).then_inc(logf_ready, 1)
            for b in range(KC):
                act.wait_ge(block_used, 28 + b + 1)
                nc.scalar.activation(KT[:, b, :], psum[:, b % 4, 0:NM], ACT.Copy).then_inc(k_out, 1)
            for hf in range(2):
                act.wait_ge(v_done, hf + 1)
                for t in range(MT):
                    nc.scalar.activation(Vm[:, t, hf * 512:(hf + 1) * 512], psum[:, 4 + 2 * hf + t, :], ACT.Copy)\
                        .then_inc(v_out, 1)
            act.wait_ge(G_ready, 1)
            nc.scalar.activation(expG, G, ACT.Exp).then_inc(expG_ready, 1)
            nc.scalar.activation(expN, G, ACT.Exp, scale=-1.0).then_inc(expG_ready, 1)
            act.wait_ge(G_ready, 2)
            nc.scalar.activation(expD, expD, ACT.Exp).then_inc(expG_ready, 1)
            act.wait_ge(conv_sum, 1)
            nc.scalar.activation(junk[:, 0:SEQ], psum[:, 4, :], ACT.Copy, scale=1.0 / CW, bias=EPS).then_inc(act_step, 1)
            act.wait_ge(act_step, 1)
            nc.scalar.activation(junk[:, SEQ:2 * SEQ], junk[:, 0:SEQ], ACT.Sqrt).then_inc(conv_root, 1)
            for h in range(HH):
                act.wait_ge(ke_tr, h + 1)
                nc.scalar.activation(keN[:, h, :], psum[:, h, :], ACT.Copy).then_inc(ke_out, 1)
            for h in range(HH):
                act.wait_ge(o_done, h + 1)
                nc.scalar.activation(sq[:, h, :], psum[:, 4 + h, :], ACT.Square).then_inc(o_sq, 1)
            for h in range(HH):
                act.wait_ge(o_sum, h + 1)
                nc.scalar.activation(rinv[:, h, :], psum[:, h, :], ACT.Copy, scale=1.0 / P, bias=EPS)\
                    .then_inc(act_step, 1)
                act.wait_ge(act_step, 2 + h)
                nc.scalar.activation(rinv[:, h, :], rinv[:, h, :], ACT.Sqrt).then_inc(o_root, 1)
            act.wait_ge(x_mixed, 8)
            norm(attn, 0)
            act.dma_start(keysT, keys_in).then_inc(ld_keys, 16)
            act.wait_ge(attn.ready, KC)
            for b in range(KC):
                act.wait_ge(block_used, 52 + b + 1)
                nc.scalar.activation(qT[:, b, :], psum[:, b % 4, :], ACT.Copy).then_inc(q_out, 1)
            for h in range(MH):
                act.wait_ge(sc_max, h + 1)
                for t in range(NT):
                    bank = 2 * (h % 2) + t // 2
                    nc.scalar.activation(prob[:, h % 2, t, :], psum[:, bank, (t % 2) * NM:(t % 2 + 1) * NM], ACT.Exp,
                                         scale=DH ** -0.5, bias=nmx[:, 4 * (h % 2) + t:4 * (h % 2) + t + 1],
                                         accum_out=den[:, 4 * (h % 2) + t:4 * (h % 2) + t + 1]).then_inc(sc_exp, 1)
                for m in range(MT):
                    act.wait_ge(p_tr, MT * h + m + 1)
                    nc.scalar.activation(pT[:, h % 2, m, :], psum[:, 4 + m, :], ACT.Copy).then_inc(pT_out, 1)
                for c in range(2):
                    act.wait_ge(ao_done, 2 * h + c + 1)
                    nc.scalar.activation(aoT[:, 2 * h + c, :], psum[:, 6 + c, :], ACT.Copy).then_inc(ao_out, 1)
            act.wait_ge(x_att, 8)
            norm(ffnn, 0)
            with act.Fori(0, 4) as r:
                for s in range(4):
                    act.wait_ge(block_used, r * 4 + (68 + s + 1))
                    nc.scalar.activation(qpT[:, bass.ds(r * 4 + s, 1), :], psum[:, s:s + 1, :], ACT.Copy)\
                        .then_inc(qp_out, 1)
            for b in range(16):
                act.wait_ge(pk_done, b + 1)
                nc.scalar.activation(score[:, b // 4, (b % 4) * 512:(b % 4 + 1) * 512], psum[:, 4 + b % 4, :], ACT.Copy)\
                    .then_inc(pk_out, 1)
            with act.Fori(0, NT) as t:
                act.wait_ge(best_ready, t + 1)
                nc.scalar.activation(ebest, ebest, ACT.Exp).then_inc(e_ready, 1)
                act.wait_ge(hk_tr, t + 1)
                nc.scalar.activation(hkT[:, :, bass.ds(t * P, P)],
                                     psum[:, 0, 0:3 * P].rearrange("p (a b) -> p a b", a=3), ACT.Copy)\
                    .then_inc(hkT_out, 1)
            for t in range(NT):
                if t >= 2:
                    act.wait_ge(stored[t % 2], 16)
                with act.Fori(0, P // TB // 2) as r:
                    for s in range(2):
                        act.wait_ge(gate_done, r * 2 + (t * (P // TB) + s + 1))
                        nc.scalar.activation(
                            stage[:, t % 2, :, bass.ds(r * (2 * TB) + s * TB, TB)].rearrange("p i n -> p n i"),
                            psum[:, 2 * s:2 * s + 2, :].rearrange("p b (n i) -> p (b n) i", i=P), ACT.Copy)\
                            .then_inc(gate_out, 1)
                act.wait_ge(gate_out, (t + 1) * (P // TB))
                act.dma_start(gate_dram[:, :, t * P:(t + 1) * P], stage[:, t % 2]).then_inc(stored[t % 2], 16)
            with act.Fori(0, GROUPS) as g:
                for t in range(GT):
                    act.wait_ge(hid_done, g * GT + (t + 1))
                    act.wait_ge(w_ready, g * GT + (t + 1))
                    nc.scalar.activation(hid[:, t % 2, :], psum[:, t % 2, :], ACT.Gelu).then_inc(gelu_out, 1)
            act.wait_ge(x_added, 8 * GROUPS + 4)
            for t in range(NT):
                nc.scalar.activation(junk, x[:, t, :], ACT.Square, accum_out=ss[:, t:t + 1]).then_inc(fin_sq, 1)
                act.wait_ge(fin_sq, t + 1)
            act.wait_ge(fin_mean, 1)
            nc.scalar.activation(rt[:, 0:NT], ms[:, 0:NT], ACT.Sqrt).then_inc(fin_root, 1)

        @block.vector
        def _(dve):
            step = Steps(dve, dve_step)
            dve.sem_inc(w_ready, 2)
            dve.sem_inc(x_added, 4)

            def norm_rows(u, col):
                dve.wait_ge(u.sumsq, u.tiles)
                nc.vector.tensor_scalar(ms[:, col:col + u.tiles], ss[:, col:col + u.tiles], 1.0 / D, EPS,
                                        ALU.mult, ALU.add).then_inc(u.mean, 1)
                dve.wait_ge(u.root, 1)
                step(nc.vector.reciprocal(rs[:, col:col + u.tiles], rt[:, col:col + u.tiles]))
                for t in range(u.tiles):
                    nc.vector.tensor_scalar(u.dst[:, t, :], u.src[:, t, :], rs[:, col + t:col + t + 1], None, ALU.mult)\
                        .then_inc(u.h, 1)

            def norm_gain(u):
                for k in range(KC):
                    dve.wait_ge(u.tr, k + 1)
                    nc.vector.tensor_scalar(u.hT[:, k, :], psum[:, 4 + k % 4, 0:u.tiles * P],
                                            vec[:, u.gain + k:u.gain + k + 1], None, ALU.mult).then_inc(u.ready, 1)

            dve.wait_ge(ld_vec, 16)
            norm_rows(mixn, 0)
            norm_gain(mixn)
            norm_rows(memn, 4)
            l0, l1 = vec[:, V_LB0:V_LB0 + HH], vec[:, V_LB1:V_LB1 + HH]
            step(nc.vector.tensor_tensor(lbm[:, 0:4], l0, l1, ALU.max))
            step(nc.vector.tensor_tensor(lbm[:, 4:8], l0, lbm[:, 0:4], ALU.subtract))
            nc.vector.tensor_tensor(lbm[:, 8:12], l1, lbm[:, 0:4], ALU.subtract).then_inc(lb_diff, 1)
            dve.wait_ge(lb_exp, 1)
            step(nc.vector.tensor_tensor(lbm[:, 12:16], lbm[:, 4:8], lbm[:, 8:12], ALU.add))
            step(nc.vector.reciprocal(lbm[:, 16:20], lbm[:, 12:16]))
            step(nc.vector.tensor_tensor(lb, lbm[:, 4:8], lbm[:, 16:20], ALU.mult))
            step(nc.vector.tensor_scalar(oml, lb, -1.0, 1.0, ALU.mult, ALU.add))
            dve.wait_ge(exp_fqg, 1)
            step(nc.vector.tensor_scalar(fgate, fgate, 1.0, None, ALU.add))
            step(nc.vector.reciprocal(fgate, fgate))
            for h in range(HH):
                step(nc.vector.tensor_scalar(fgate[:, h, :], fgate[:, h, :], oml[:, h:h + 1], lb[:, h:h + 1],
                                             ALU.mult, ALU.add))
            dve.wait_ge(memn.h, MT)
            nc.vector.tensor_scalar(kk, fgate, -1.0, 1.0, ALU.mult, ALU.add).then_inc(fg_ready, 1)
            for n, (a, b) in enumerate(((qsil, pQ), (gsil, pG))):
                dve.wait_ge(exp_fqg, n + 2)
                step(nc.vector.tensor_scalar(a, a, 1.0, None, ALU.add))
                step(nc.vector.reciprocal(a, a))
                step(nc.vector.tensor_tensor(a, a, b, ALU.mult))
            norm_gain(memn)
            dve.wait_ge(consts, 5)
            dve.wait_ge(logf_ready, 1)
            for h in range(HH):
                step(nc.vector.tensor_tensor_scan(G[:, h, :], reset, logf[:, h, :], 0.0, ALU.mult, ALU.add))
            nc.vector.tensor_copy(expD[:, 0, 0:1], G[:, 0, 0:1]).then_inc(G_ready, 1)
            dve.wait_ge(G_ready, 1)
            Gc = G.rearrange("p h (c t) -> p (h c) t", t=CH)
            nc.vector.tensor_tensor(expD.rearrange("p h (c t) -> p (h c) t", t=CH),
                                    Gc[:, :, CH - 1:CH].to_broadcast([P, HH * NCH, CH]), Gc, ALU.subtract)\
                .then_inc(G_ready, 1)
            dve.wait_ge(expG_ready, 1)
            step(nc.vector.tensor_copy(decay, expG.rearrange("p h (c t) -> p h c t", t=CH)[:, :, :, CH - 1]))
            step(nc.vector.tensor_tensor(pQ, qsil, expG, ALU.mult))
            dve.wait_ge(expG_ready, 3)
            step(nc.vector.tensor_tensor(pF, kk, expN, ALU.mult))
            nc.vector.tensor_tensor(expD, kk, expD, ALU.mult).then_inc(qk_ready, 1)
            for c in range(CC):
                cw = [vec[:, V_CW + CC * j + c:V_CW + CC * j + c + 1] for j in range(3)]
                y, u = yT[:, c, :], pC[:, c, :]
                step(nc.vector.tensor_tensor(u, u, pV[:, c, :], ALU.mult))
                step(nc.vector.tensor_scalar(y, u, cw[2], None, ALU.mult))
                step(nc.vector.scalar_tensor_tensor(y[:, 1:], u[:, :SEQ - 1], cw[1], y[:, 1:], ALU.mult, ALU.add))
                step(nc.vector.scalar_tensor_tensor(y[:, 2:], u[:, :SEQ - 2], cw[0], y[:, 2:], ALU.mult, ALU.add))
                step(nc.vector.tensor_tensor(y, y, pB[:, c, :], ALU.mult))
                if c == 0:
                    dve.wait_ge(memn.tr, KC)
                nc.vector.tensor_tensor(csq[:, c, :], y, y, ALU.mult).then_inc(conv_sq, 1)
            dve.wait_ge(conv_root, 1)
            step(nc.vector.reciprocal(junk[:, 0:SEQ], junk[:, SEQ:2 * SEQ]))
            for c in range(CC):
                nc.vector.scalar_tensor_tensor(yT[:, c, :], yT[:, c, :], vec[:, V_CONV + c:V_CONV + c + 1],
                                               junk[:, 0:SEQ], ALU.mult, ALU.mult).then_inc(conv_y, 1)
            step(nc.vector.memset(aT, 0.0))
            for h in range(HH):
                dve.wait_ge(a_done, h + 1)
                nc.vector.copy_predicated(
                    aT[:, h, :].rearrange("p (t c) -> p t c", c=P),
                    causal.bitcast(U32).rearrange("p (a c) -> p a c", a=1).to_broadcast([P, NT, P]),
                    psum[:, 4 + h, :].rearrange("p (t c) -> p t c", c=P)).then_inc(a_ready, 1)
            for h in range(HH):
                dve.wait_ge(u_done, h + 1)
                for n in range(NCH - 1):
                    u = psum[:, 2 * (h % 2) + n % 2, (n // 2) * P:(n // 2 + 1) * P]
                    if n == 0:
                        ins = nc.vector.tensor_copy(S[:, h, 1, :], u)
                    else:
                        ins = nc.vector.scalar_tensor_tensor(S[:, h, n + 1, :], S[:, h, n, :], decay[:, h, n:n + 1], u,
                                                             ALU.mult, ALU.add)
                    ins.then_inc(s_ready, 1)
                    dve.wait_ge(s_ready, h * (NCH - 1) + n + 1)
            for h in range(HH):
                dve.wait_ge(o_root, h + 1)
                step(nc.vector.reciprocal(rinv[:, h, :], rinv[:, h, :]))
                step(nc.vector.scalar_tensor_tensor(rinv[:, h, :], rinv[:, h, :], vec[:, V_HGRN + h:V_HGRN + h + 1],
                                                    gsil[:, h, :], ALU.mult, ALU.mult))
                nc.vector.tensor_tensor(yT[:, CC + h, :], rinv[:, h, :], psum[:, 4 + h, :], ALU.mult).then_inc(y_ready, 1)

            def residual(done, added):
                for hf in range(2):
                    dve.wait_ge(done, hf + 1)
                    for t in range(NT):
                        nc.vector.tensor_tensor(x[:, t, hf * 512:(hf + 1) * 512], x[:, t, hf * 512:(hf + 1) * 512],
                                                psum[:, 4 * hf + t, :], ALU.add).then_inc(added, 1)

            residual(mix_done, x_mixed)
            dve.wait_ge(x_mixed, 8)
            norm_rows(attn, 0)
            norm_gain(attn)
            for h in range(MH):
                o = 4 * (h % 2)
                dve.wait_ge(sc_done, h + 1)
                step(nc.vector.tensor_reduce(mx[:, o:o + NT].rearrange("p (a b) -> p a b", a=2),
                                             psum[:, 2 * (h % 2):2 * (h % 2) + 2, :].rearrange("p a (b m) -> p a b m", b=2),
                                             AX_X, ALU.max))
                nc.vector.tensor_scalar(nmx[:, o:o + NT], mx[:, o:o + NT], -DH ** -0.5, None, ALU.mult).then_inc(sc_max, 1)
                dve.wait_ge(sc_exp, NT * (h + 1))
                step(nc.vector.reciprocal(rden[:, o:o + NT], den[:, o:o + NT]))
                for t in range(NT):
                    nc.vector.tensor_scalar(prob[:, h % 2, t, :], prob[:, h % 2, t, :], rden[:, o + t:o + t + 1], None,
                                            ALU.mult).then_inc(p_ready, 1)
            residual(att_done, x_att)
            dve.wait_ge(x_att, 8)
            norm_rows(ffnn, 0)
            norm_gain(ffnn)

            def top16(values, vals, index):
                step(nc.vector.max(vals[:, 0:8], values))
                step(nc.vector.max_index(index[:, 0:8], vals[:, 0:8], values))
                step(nc.vector.match_replace(values, vals[:, 0:8], values, NEG))
                step(nc.vector.max(vals[:, 8:16], values))
                step(nc.vector.max_index(index[:, 8:16], vals[:, 8:16], values))

            dve.wait_ge(pk_out, 16)
            for t in range(NT):
                for j in range(16):
                    top16(score[:, t, j * NK:(j + 1) * NK], top[:, j, :], topi[:, j, :].bitcast(U32))
                step(nc.vector.tensor_copy(topf, topi.bitcast(U32)))
                half = top.rearrange("p (h q) k -> p h q k", q=2)
                step(nc.vector.tensor_tensor(
                    cand.rearrange("p h (a b) -> p h a b", a=TK),
                    half[:, :, 0, :].rearrange("p h (a b) -> p h a b", b=1).to_broadcast([P, PH, TK, TK]),
                    half[:, :, 1, :].rearrange("p h (a b) -> p h a b", a=1).to_broadcast([P, PH, TK, TK]), ALU.add))
                for h in range(PH):
                    top16(cand[:, h, :], best[:, h, :], pos[:, h, :].bitcast(U32))
                nc.vector.tensor_tensor(ebest, best, best[:, :, 0:1].to_broadcast([P, PH, TK]), ALU.subtract)\
                    .then_inc(best_ready, 1)
                step(nc.vector.tensor_scalar(posd.bitcast(U32), pos.bitcast(U32), 4, None, ALU.logical_shift_right))
                step(nc.vector.tensor_copy(posf[:, 0], posd.bitcast(U32)))
                step(nc.vector.tensor_scalar(posd.bitcast(U32), pos.bitcast(U32), TK - 1, None, ALU.bitwise_and))
                step(nc.vector.tensor_copy(posf[:, 1], posd.bitcast(U32)))
                halff = topf.rearrange("p (h q) k -> p h q k", q=2)
                for q in range(2):
                    step(nc.vector.tensor_tensor(
                        onehot.rearrange("p h (k a) -> p (h k) a", a=TK),
                        posf[:, q].rearrange("p h (k b) -> p (h k) b", b=1).to_broadcast([P, PH * TK, TK]),
                        iota[:, 0:TK].rearrange("p (b a) -> p b a", b=1).to_broadcast([P, PH * TK, TK]), ALU.is_equal))
                    step(nc.vector.tensor_tensor(
                        picked.rearrange("p h (k a) -> p h k a", a=TK),
                        onehot.rearrange("p h (k a) -> p h k a", a=TK),
                        halff[:, :, q, :].rearrange("p h (b a) -> p h b a", b=1).to_broadcast([P, PH, TK, TK]), ALU.mult))
                    step(nc.vector.tensor_reduce(hk[:, q, :], picked.rearrange("p h (k a) -> p (h k) a", a=TK),
                                                 AX_X, ALU.add))
                dve.wait_ge(e_ready, t + 1)
                step(nc.vector.tensor_reduce(esum[:, 0:PH], ebest, AX_X, ALU.add))
                step(nc.vector.reciprocal(esum[:, 8:16], esum[:, 0:8]))
                nc.vector.tensor_tensor(hk[:, 2, :].rearrange("p (h k) -> p h k", k=TK), ebest,
                                        esum[:, 8:16].rearrange("p (h k) -> p h k", k=1).to_broadcast([P, PH, TK]),
                                        ALU.mult).then_inc(hk_ready, 1)
                dve.wait_ge(hkT_out, t + 1)

            def hots(n, s):
                for j in range(TB):
                    nc.vector.tensor_scalar(hot[:, s, 0, j * P:(j + 1) * P], iota, hkT[:, 0, bass.ds(n + j, 1)], None,
                                            ALU.is_equal)
                    ins = nc.vector.tensor_scalar(hot[:, s, 1, j * P:(j + 1) * P], iota, hkT[:, 1, bass.ds(n + j, 1)],
                                                  hkT[:, 2, bass.ds(n + j, 1)], ALU.is_equal, ALU.mult)
                ins.then_inc(hot_ready, 1)

            for s in range(2):
                hots(s * TB, s)
            with dve.Fori(1, SEQ // TB // 2) as r:
                for s in range(2):
                    dve.wait_ge(gate_done, r * 2 + (s - 1))
                    hots(r * (2 * TB) + s * TB, s)

            def weigh(g, s):
                dve.wait_ge(ld_gate[s], ld_count(g, s))
                for t in range(GT):
                    dve.wait_ge(gelu_out, g * GT + (t + 3))
                    nc.vector.tensor_tensor(wgt[:, s, t, :], hid[:, t % 2, :], gates[:, s, t, :], ALU.mult)\
                        .then_inc(w_ready, 1)

            def accumulate(g):
                for o in range(8):
                    dve.wait_ge(up_done, g * 8 + (o + 1))
                    xs = x[:, o // 2, (o % 2) * 512:(o % 2 + 1) * 512]
                    nc.vector.tensor_tensor(xs, xs, psum[:, 4 + o % 4, :], ALU.add).then_inc(x_added, 1)

            weigh(0, 0)
            weigh(1, 1)
            accumulate(0)
            with dve.Fori(1, GROUPS // 2) as r:
                weigh(r * 2, 0)
                accumulate(r * 2 - 1)
                weigh(r * 2 + 1, 1)
                accumulate(r * 2)
            accumulate(GROUPS - 1)
            dve.wait_ge(fin_sq, NT)
            nc.vector.tensor_scalar(ms[:, 0:NT], ss[:, 0:NT], 1.0 / D, EPS, ALU.mult, ALU.add).then_inc(fin_mean, 1)
            dve.wait_ge(fin_root, 1)
            step(nc.vector.reciprocal(rs[:, 0:NT], rt[:, 0:NT]))
            dve.wait_ge(ld_fin, 16)
            for t in range(NT):
                nc.vector.scalar_tensor_tensor(hn[:, t, :], x[:, t, :], rs[:, t:t + 1], fin_w, ALU.mult, ALU.mult)\
                    .then_inc(fin_y, 1)

        @block.tensor
        def _(pe):
            pe.wait_ge(consts, 5)

            def turn(u):
                pe.wait_ge(u.h, u.tiles)
                for k in range(KC):
                    if k >= 4:
                        pe.wait_ge(u.ready, k - 3)
                    for t in range(u.tiles):
                        ins = nc.tensor.transpose(psum[:, 4 + k % 4, t * P:(t + 1) * P], u.dst[:, t, k * P:(k + 1) * P], ident)
                    ins.then_inc(u.tr, 1)

            def columns(s, turns, rhs, n):
                pe.wait_ge(wt[s], turns)
                for k in range(KC):
                    ins = nc.tensor.matmul(psum[:, s, 0:n], ring[:, s, k * P:(k + 1) * P], rhs[:, k, :],
                                           start=(k == 0), stop=(k == KC - 1))
                ins.then_inc(block_used, 1)

            def rows(s, turns, lhs, banks, k0, last=None):
                pe.wait_ge(wt[s], turns)
                for j in range(2):
                    for n, bank in enumerate(banks):
                        ins = nc.tensor.matmul(psum[:, bank, :], lhs[:, k0 + j, n * P:(n + 1) * P],
                                               ring[:, s, j * 512:(j + 1) * 512],
                                               start=(k0 + j == 0), stop=(k0 + j == KC - 1))
                ins.then_inc(block_used, 1)

            turn(mixn)
            pe.wait_ge(mixn.ready, KC)
            with pe.Fori(0, 6) as r:
                for s in range(4):
                    pe.wait_ge(bank_free, r * 4 + (s + 1))
                    columns(s, r * 16 + 16, hT, SEQ)
            for s in range(4):
                rows(s, 16 * 7, hT, range(4, 8), 2 * s)
            pe.wait_ge(block_used, 28)
            pe.sem_inc(i_done, 1)
            pe.wait_ge(i_out, NT)
            turn(memn)
            pe.wait_ge(memn.ready, KC)
            pe.wait_ge(bank_free, 28)
            for b in range(KC):
                if b >= 4:
                    pe.wait_ge(k_out, b - 3)
                columns(b % 4, 16 * (8 + b // 4), memT, NM)
            for hf in range(2):
                for s in range(4):
                    rows(s, 16 * (10 + hf), memT, range(4 + 2 * hf, 6 + 2 * hf), 2 * s)
                pe.wait_ge(block_used, 40 + 4 * hf)
                pe.sem_inc(v_done, 1)
            pe.wait_ge(v_out, 2 * MT)
            pe.wait_ge(conv_sq, CC)
            for c in range(CC):
                ins = nc.tensor.matmul(psum[:, 4, :], ones, csq[:, c, :], start=(c == 0), stop=(c == CC - 1))
            ins.then_inc(conv_sum, 1)
            pe.wait_ge(qk_ready, 1)
            pe.wait_ge(k_out, KC)
            for h in range(HH):
                for t in range(NT):
                    ins = nc.tensor.transpose(psum[:, h, t * P:(t + 1) * P], expD[:, h, t * P:(t + 1) * P], ident)
                ins.then_inc(ke_tr, 1)
            pe.wait_ge(conv_y, CC)
            for h in range(HH):
                for t in range(NT):
                    ins = nc.tensor.matmul(psum[:, 4 + h, t * P:(t + 1) * P], pF[:, h, t * P:(t + 1) * P],
                                           pQ[:, h, t * P:(t + 1) * P], start=True, stop=True)
                ins.then_inc(a_done, 1)
            for h in range(HH):
                pe.wait_ge(ke_out, HH)
                if h >= 2:
                    pe.wait_ge(s_ready, (h - 1) * (NCH - 1))
                for n in range(NCH - 1):
                    lo = (n % 2) * CH
                    ins = nc.tensor.matmul(psum[:, 2 * (h % 2) + n % 2, (n // 2) * P:(n // 2 + 1) * P],
                                           keN[lo:lo + CH, h, (n // 2) * P:(n // 2 + 1) * P],
                                           iN[lo:lo + CH, n // 2, h * P:(h + 1) * P], start=True, stop=True)
                ins.then_inc(u_done, 1)
            for h in range(HH):
                pe.wait_ge(a_ready, h + 1)
                pe.wait_ge(s_ready, (h + 1) * (NCH - 1))
                for t in range(NT):
                    nc.tensor.matmul(psum[:, 4 + h, t * P:(t + 1) * P], iN[:, t, h * P:(h + 1) * P],
                                     aT[:, h, t * P:(t + 1) * P], start=True, stop=False, skip_group_check=True)
                    for n in (2 * t, 2 * t + 1):
                        if n == 0:
                            continue
                        ins = nc.tensor.matmul(psum[:, 4 + h, n * CH:(n + 1) * CH], S[:, h, n, :],
                                               pQ[:, h, n * CH:(n + 1) * CH], start=False, stop=(n % 2 == 1),
                                               skip_group_check=True)
                ins.then_inc(o_done, 1)
            for h in range(HH):
                pe.wait_ge(o_sq, h + 1)
                nc.tensor.matmul(psum[:, h, :], ones, sq[:, h, :], start=True, stop=True).then_inc(o_sum, 1)

            def product(lhs, turn0, done, first):
                for hf in range(2):
                    pe.wait_ge(*first[hf])
                    for s in range(4):
                        rows(s, 16 * (turn0 + hf), lhs, range(4 * hf, 4 * hf + 4), 2 * s)
                    pe.wait_ge(block_used, 4 * (turn0 + hf))
                    pe.sem_inc(done, 1)

            pe.wait_ge(y_ready, HH)
            product(yT, 12, mix_done, ((o_root, HH), (y_ready, HH)))
            turn(attn)
            pe.wait_ge(attn.ready, KC)
            for b in range(KC):
                if b >= 4:
                    pe.wait_ge(q_out, b - 3)
                columns(b % 4, 16 * (14 + b // 4), hT, SEQ)
            pe.wait_ge(q_out, KC)
            for h in range(MH):
                if h >= 2:
                    pe.wait_ge(sc_exp, NT * (h - 1))
                for t in range(NT):
                    for c in range(2):
                        ins = nc.tensor.matmul(psum[:, 2 * (h % 2) + t // 2, (t % 2) * NM:(t % 2 + 1) * NM],
                                               qT[:, 2 * h + c, t * P:(t + 1) * P], KT[:, 2 * h + c, :],
                                               start=(c == 0), stop=(c == 1), skip_group_check=True)
                ins.then_inc(sc_done, 1)
                pe.wait_ge(p_ready, NT * (h + 1))
                for m in range(MT):
                    if h:
                        pe.wait_ge(pT_out, MT * (h - 1) + m + 1)
                    for t in range(NT):
                        ins = nc.tensor.transpose(psum[:, 4 + m, t * P:(t + 1) * P], prob[:, h % 2, t, m * P:(m + 1) * P], ident)
                    ins.then_inc(p_tr, 1)
                pe.wait_ge(pT_out, MT * (h + 1))
                for c in range(2):
                    if h:
                        pe.wait_ge(ao_out, 2 * (h - 1) + c + 1)
                    for m in range(MT):
                        ins = nc.tensor.matmul(psum[:, 6 + c, :], Vm[:, m, h * DH + c * P:h * DH + (c + 1) * P],
                                               pT[:, h % 2, m, :], start=(m == 0), stop=(m == MT - 1))
                    ins.then_inc(ao_done, 1)
            pe.wait_ge(ao_out, 2 * MH)
            product(aoT, 16, att_done, ((sc_exp, NT * MH), (ao_out, 2 * MH)))
            turn(ffnn)
            pe.wait_ge(ffnn.ready, KC)
            for s in range(4):
                columns(s, 16 * 18, hT, SEQ)
            with pe.Fori(1, 4) as r:
                for s in range(4):
                    pe.wait_ge(qp_out, r * 4 + (s - 3))
                    columns(s, r * 16 + 16 * 18, hT, SEQ)
            pe.wait_ge(ld_keys, 16)
            pe.wait_ge(qp_out, 16)
            for b in range(16):
                if b >= 4:
                    pe.wait_ge(pk_out, b - 3)
                for j in range(4):
                    hp = 4 * (b % 4) + j
                    ins = nc.tensor.matmul(psum[:, 4 + b % 4, j * NK:(j + 1) * NK], qpT[:, hp, (b // 4) * P:(b // 4 + 1) * P],
                                           keysT[:, hp, :], start=True, stop=True)
                ins.then_inc(pk_done, 1)
            with pe.Fori(0, NT) as t:
                pe.wait_ge(hk_ready, t + 1)
                for j in range(3):
                    ins = nc.tensor.transpose(psum[:, 0, j * P:(j + 1) * P], hk[:, j, :], ident)
                ins.then_inc(hk_tr, 1)

            def gate_step(n, s):
                pe.wait_ge(hot_ready, n + 1)
                for j in range(TB):
                    ins = nc.tensor.matmul(psum[:, 2 * s + j // 4, (j % 4) * P:(j % 4 + 1) * P],
                                           hot[:, s, 1, j * P:(j + 1) * P], hot[:, s, 0, j * P:(j + 1) * P],
                                           start=True, stop=True)
                ins.then_inc(gate_done, 1)

            pe.wait_ge(hkT_out, NT)
            for s in range(2):
                gate_step(s, s)
            with pe.Fori(1, SEQ // TB // 2) as r:
                for s in range(2):
                    pe.wait_ge(gate_out, r * 2 + (s - 1))
                    gate_step(r * 2 + s, s)
            pe.wait_ge(gate_out, SEQ // TB)

            def first_product(g, s):
                pe.wait_ge(ld_down[s], ld_count(g, s))
                for t in range(GT):
                    pe.wait_ge(gelu_out, g * GT + (t + 1))
                    for k in range(KC):
                        ins = nc.tensor.matmul(psum[:, t % 2, :], down[:, s, t, k * P:(k + 1) * P], hT[:, k, :],
                                               start=(k == 0), stop=(k == KC - 1))
                    ins.then_inc(hid_done, 1)

            def second_product(g, s):
                pe.wait_ge(ld_up[s], ld_count(g, s))
                pe.wait_ge(w_ready, g * GT + (GT + 2))
                for o in range(8):
                    pe.wait_ge(x_added, g * 8 + (o + 1))
                    for t in range(GT):
                        ins = nc.tensor.matmul(psum[:, 4 + o % 4, :], wgt[:, s, t, (o // 2) * P:(o // 2 + 1) * P],
                                               up[:, s, t, (o % 2) * 512:(o % 2 + 1) * 512],
                                               start=(t == 0), stop=(t == GT - 1))
                    ins.then_inc(up_done, 1)

            first_product(0, 0)
            first_product(1, 1)
            second_product(0, 0)
            with pe.Fori(1, GROUPS // 2) as r:
                first_product(r * 2, 0)
                second_product(r * 2 - 1, 1)
                first_product(r * 2 + 1, 1)
                second_product(r * 2, 0)
            second_product(GROUPS - 1, 1)


def ld_count(g, s):
    return g * 8 + (16 - 8 * s)


def kernel(**inputs):
    import numpy as np
    import concourse.bacc as bacc
    from concourse.bass_utils import run_bass_kernel_spmd

    def cols(w):
        return w.reshape(KC, P, -1, P).transpose(2, 1, 0, 3).reshape(-1, P, D)

    def rws(w):
        return w.reshape(4, 2, P, -1, 512).transpose(3, 0, 2, 1, 4).reshape(-1, P, D)

    def vec(v):
        return v.reshape(-1, P).T

    i = {k: np.asarray(v) for k, v in inputs.items()}
    w_in, wkv = i["w_in"][0], i["wkv_mem"][0]
    o0 = 3 * CW
    front = np.ascontiguousarray(np.concatenate([
        cols(w_in[:, :o0 + 2 * CW]), cols(w_in[:, o0 + 3 * CW:]), rws(w_in[:, o0 + 2 * CW:o0 + 3 * CW]),
        cols(wkv[:, :D]), rws(wkv[:, D:]), rws(i["w_out"][0]), cols(i["wq_mem"][0]), rws(i["wo_mem"][0]),
        cols(i["peer_w_query"][0])]))
    vecs = np.ascontiguousarray(np.concatenate([
        vec(i["mix_norm_w"][0]), vec(i["conv_norm_w"][0]), vec(i["hgrn_norm_w"][0]), vec(i["hgrn_lb_logits"][0]),
        vec(i["hgrn_lb_logits"][1]), vec(i["xattn_norm_w"][0]), vec(i["mem_norm_w"][0]), vec(i["ffn_norm_w"][0]),
        vec(i["conv_w"][0].reshape(-1))], axis=1))
    down = i["peer_down"][0].reshape(NK, P, KC, P).transpose(0, 3, 2, 1).reshape(GROUPS, GT, P, D)
    arrays = {
        "x_in": i["x"][0], "mem_in": i["mem"][0], "vecs_in": vecs, "final_in": i["final_norm_w"].reshape(1, D),
        "front_w": front, "keys_in": i["peer_sub_keys"][0].reshape(16, NK, P).transpose(2, 0, 1),
        "down_in": down, "up_in": i["peer_up"][0].reshape(GROUPS, GT, P, D)}
    arrays = {k: np.ascontiguousarray(v) for k, v in arrays.items()}
    nc = bacc.Bacc("TRN2", target_bir_lowering=False, num_devices=1)
    args = [nc.dram_tensor(k, v.shape, mybir.dt.from_np(v.dtype), kind="ExternalInput").ap() for k, v in arrays.items()]
    args.append(nc.dram_tensor("out", (SEQ, D), F32, kind="ExternalOutput").ap())
    args.append(nc.dram_tensor("gate_dram", (P, NK, SEQ), F32, kind="Internal").ap())
    build(nc, *args)
    r = run_bass_kernel_spmd(nc, [arrays], core_ids=[0])
    return r.results[0]["out"].reshape(1, SEQ, D)
```

```python
from contextlib import ExitStack

import concourse.bass as bass
from concourse import mybir

F32 = mybir.dt.float32
F32R = mybir.dt.float32r
U32 = mybir.dt.uint32
ALU = mybir.AluOpType
ACT = mybir.ActivationFunctionType
AX_X = mybir.AxisListType.X

P = 128
D = 1024
KC = D // P
SEQ = 512
NT = SEQ // P
NM = 256
MT = NM // P
CW = 512
CC = CW // P
HH = 4
CH = 64
NCH = SEQ // CH
MH = 4
DH = D // MH
PH = 8
NK = 128
TK = 16
NEG = -3.0e38
EPS = 1e-6

RING = 4
FRONT = 84
AHEAD = 8
EARLY = AHEAD * 4 + 8
GT = 2
GROUPS = NK // GT
FIRST_D = EARLY // GT - 1
TB = 8

V_MIX, V_CONV, V_HGRN, V_LB0, V_LB1, V_ATT, V_MEM, V_FFN, V_CW = 0, 8, 12, 16, 20, 24, 32, 40, 48
NV = V_CW + 3 * CC


def build(nc, x_in, mem_in, vecs_in, final_in, front_w, keys_in, down_in, up_in, out, gate_dram, hid_dram):
    ctx = ExitStack()
    with ctx:
        def sem(name):
            return ctx.enter_context(nc.semaphore(name))

        KB = 256
        with ExitStack() as over:
            def halves(name, kb, shape, now):
                if kb > now:
                    over.enter_context(nc.sbuf_tensor(f"pad{kb}", [P, (kb - now) * KB], F32))
                return [over.enter_context(nc.sbuf_tensor(name + half, [P] + shape, F32R)) for half in ("_high", "_low")]

            w_half = halves("w", 44, [2, D], 0)
            hT_half = halves("hT", 60, [KC, SEQ], 60)
            up_half = halves("up", 140, [4, D], 92)
            wgt_half = halves("wgt", 172, [4, SEQ], 172)
            memT_half = halves("memT", 188, [KC, NM], 188)
        kept = ctx.enter_context(nc.sbuf_tensor("kept", [P, 44 * KB], F32))
        ctx.enter_context(nc.sbuf_tensor("under_w", [P, 16 * KB], F32))
        arena = ctx.enter_context(nc.sbuf_tensor("arena", [P, 146 * KB], F32))
        psum = ctx.enter_context(nc.psum_tensor("psum", [P, 8, 512], F32))

        def at(kb, n, *dims):
            where, kb = (kept, kb) if kb < 44 else (arena, kb - 60)
            a = where[:, int(kb * KB):int(kb * KB) + n]
            if len(dims) == 2:
                return a.rearrange("p (a b) -> p a b", a=dims[0])
            if len(dims) == 3:
                return a.rearrange("p (a b c) -> p a b c", a=dims[0], b=dims[1])
            return a

        x = at(0, NT * D, NT, D)
        vec = at(16, NV)
        ident = at(16.5, P)
        ones = at(17, P)
        iota = at(17.5, P)
        causal = at(18, P)
        fin_w = at(18.5, D)
        ss = at(22.5, 16)
        ms = at(22.5625, 16)
        rt = at(22.625, 16)
        rs = at(22.6875, 16)
        lbm = at(22.75, 32)
        lb, oml = lbm[:, 20:24], lbm[:, 24:28]
        decay = at(23, HH * NCH, HH, NCH)
        mx, nmx, den, rden = (at(23.25 + 0.0625 * j, 16) for j in range(4))
        junk = at(23.5, D)
        ring = at(28, RING * D, RING, D)
        hn = at(92, NT * D, NT, D)
        proj = at(108, 24 * SEQ, 24, SEQ)
        pB, pC, pV, pQ, pF, pG = (proj[:, 4 * j:4 * j + 4, :] for j in range(6))
        iN = at(156, NT * CW, NT, CW)
        mem = at(164, MT * D, MT, D)
        KT = at(172, KC * NM, KC, NM)
        Vm = at(180, MT * D, MT, D)
        kk = at(92, HH * SEQ, HH, SEQ)
        G = at(100, HH * SEQ, HH, SEQ)
        expD = at(60, HH * SEQ, HH, SEQ)
        expN = at(68, HH * SEQ, HH, SEQ)
        csq = at(76, CC * SEQ, CC, SEQ)
        aT = pC
        keN = pV
        S = at(92, HH * NCH * P, HH, NCH, P)
        sq = at(188, HH * SEQ, HH, SEQ)
        rinv = at(196, HH * SEQ, HH, SEQ)
        reset = at(204, SEQ)
        qT = at(108, KC * SEQ, KC, SEQ)
        prob = at(124, 2 * NT * NM, 2, NT, NM)
        pT = at(132, 2 * MT * SEQ, 2, MT, SEQ)
        qpT = at(108, 16 * SEQ, 16, SEQ)
        score = at(140, NT * 16 * NK, NT, 16 * NK)
        keysT = at(172, 16 * NK, 16, NK)
        cand = at(108, PH * TK * TK, PH, TK * TK)
        onehot = at(116, PH * TK * TK, PH, TK * TK)
        top = at(124, 16 * TK, 16, TK)
        topi = at(125, 16 * TK, 16, TK)
        topf = at(126, 16 * TK, 16, TK)
        best = at(127, PH * TK, PH, TK)
        pos = at(127.5, PH * TK, PH, TK)
        posd = at(128, PH * TK, PH, TK)
        posf = at(128.5, 2 * PH * TK, 2, PH, TK)
        ebest = at(129.5, PH * TK, PH, TK)
        hk = at(130, 3 * P, 3, P)
        esum = at(131.5, 16)
        hkT = at(132, 3 * SEQ, 3, SEQ)
        hid = [at(138, SEQ), at(204, SEQ)]
        hot = at(92, 2 * 2 * TB * P, 2, 2, TB * P)
        stage = at(140, 2 * P * CH, 2, P, CH)
        uraw = at(92, 4 * D, 4, D)
        wraw = at(108, 2 * SEQ, 2, SEQ)
        gates = at(188, 4 * SEQ, 4, SEQ)
        hidr = at(196, 4 * SEQ, 4, SEQ)

        ld_x, ld_mem, ld_vec, ld_fin, ld_keys = (sem(n) for n in ("ld_x", "ld_mem", "ld_vec", "ld_fin", "ld_keys"))
        wt = [sem(f"weight_slot{s}") for s in range(RING)]
        block_used = sem("block_used")
        high_ready = sem("high_ready")
        low_ready = sem("low_ready")
        up_high, up_low = sem("up_high"), sem("up_low")
        consts = sem("consts")
        class Norm:
            def __init__(self, name, src, dst, hT, tiles, gain):
                self.src, self.dst, self.hT, self.tiles, self.gain = src, dst, hT, tiles, gain
                self.sumsq, self.mean, self.root, self.h, self.tr, self.ready = (
                    sem(f"{name}_{s}") for s in ("sumsq", "mean", "root", "h", "transposed", "ready"))

        mixn = Norm("mix", x, hn, hT_half, NT, V_MIX)
        memn = Norm("mem", mem, mem, memT_half, MT, V_MEM)
        attn = Norm("att", x, hn, hT_half, NT, V_ATT)
        ffnn = Norm("ffn", x, hn, hT_half, NT, V_FFN)
        bank_free = sem("bank_free")
        i_out, k_out, v_out = sem("i_out"), sem("k_out"), sem("v_out")
        i_done, v_done = sem("i_done"), sem("v_done")
        lb_diff, lb_exp = sem("lb_diff"), sem("lb_exp")
        exp_fqg, fg_ready, logf_ready, G_ready, expG_ready, qk_ready = (
            sem(n) for n in ("exp_fqg", "fg_ready", "logf_ready", "G_ready", "expG_ready", "qk_ready"))
        conv_sq, conv_sum, conv_root = (sem(n) for n in ("conv_sq", "conv_sum", "conv_root"))
        ke_tr, ke_out, a_done, a_ready = (sem(n) for n in ("ke_tr", "ke_out", "a_done", "a_ready"))
        u_done, u_used, s_ready, o_done, o_sq, o_sum, o_root = (
            sem(n) for n in ("u_done", "u_used", "s_ready", "o_done", "o_sq", "o_sum", "o_root"))
        mix_done, x_mixed = sem("mix_done"), sem("x_mixed")
        q_out, sc_done, sc_max, sc_exp, p_ready, p_tr, pT_out, ao_done, ao_out = (
            sem(n) for n in ("q_out", "sc_done", "sc_max", "sc_exp", "p_ready", "p_tr", "pT_out", "ao_done", "ao_out"))
        att_done, x_att = sem("att_done"), sem("x_att")
        qp_out, pk_done, pk_out = sem("qp_out"), sem("pk_done"), sem("pk_out")
        best_ready, e_ready, hk_ready, hk_tr, hkT_out = (
            sem(n) for n in ("best_ready", "e_ready", "hk_ready", "hk_tr", "hkT_out"))
        hot_ready, gate_done, gate_out = (sem(n) for n in ("hot_ready", "gate_done", "gate_out"))
        stored = [sem(f"gates_stored{s}") for s in range(2)]
        ld_up = [sem(f"ld_up{s}") for s in range(4)]
        ld_gate = [sem(f"ld_gate{s}") for s in range(4)]
        ld_hid = [sem(f"ld_hid{s}") for s in range(4)]
        hid_stored = [sem(f"hid_stored{s}") for s in range(2)]
        gelu_out, w_raw, w_high, w_ready, up_done, x_added = (
            sem(n) for n in ("gelu_out", "w_raw", "w_high", "w_ready", "up_done", "x_added"))
        ao_high, conv_y, y_ready = sem("ao_high"), sem("conv_y"), sem("y_ready")
        fin_sq, fin_mean, fin_root, fin_y, out_stored = (
            sem(n) for n in ("fin_sq", "fin_mean", "fin_root", "fin_y", "out_stored"))
        dve_step, act_step, pool_step = sem("dve_step"), sem("act_step"), sem("pool_step")

        class Steps:
            def __init__(self, eng, own):
                self.eng, self.own, self.n = eng, own, 0

            def put(self, ins):
                ins.then_inc(self.own, 1)
                self.n += 1

            def end(self):
                self.eng.wait_ge(self.own, self.n)

            def __call__(self, ins):
                self.put(ins)
                self.end()

        block = ctx.enter_context(nc.Block())

        @block.sync
        def _(sp):
            def load_block(b, s):
                sp.dma_start(ring[:, s, :], front_w[bass.ds(b, 1)].rearrange("b p n -> (b p) n")).then_inc(wt[s], 16)

            def load_down(i, s):
                sp.dma_start(ring[:, s, :], down_in[bass.ds(i, 1)].rearrange("b p n -> (b p) n")).then_inc(wt[s], 16)

            for s in range(RING):
                load_block(s, s)
            with sp.Fori(1, FRONT // RING) as r:
                for s in range(RING):
                    sp.wait_ge(low_ready, r * RING + (s + 1 - RING))
                    load_block(r * RING + s, s)
            with sp.Fori(0, EARLY // RING + 1) as r:
                for s in range(RING):
                    sp.wait_ge(low_ready, r * RING + (FRONT + s + 1 - RING))
                    load_down(r * RING + s, s)

            def load_up(i, s):
                sp.dma_start(uraw[:, s, :], up_in[bass.ds(i, 1)].rearrange("b p n -> (b p) n")).then_inc(ld_up[s], 16)

            def load_gates(i, s):
                sp.dma_start(gates[:, s, :], gate_dram[:, bass.ds(i, 1), :].rearrange("p a n -> p (a n)"))\
                    .then_inc(ld_gate[s], 16)

            def load_hid(i, s):
                sp.dma_start(hidr[:, s, :], hid_dram[bass.ds(i, 1)].rearrange("b p n -> (b p) n")).then_inc(ld_hid[s], 16)

            sp.wait_ge(gate_done, SEQ // TB)
            for s in range(4):
                load_up(s, s)
            for s in range(2):
                sp.wait_ge(stored[s], 16 * NT)
                sp.wait_ge(hid_stored[s], 16 * EARLY // 2)
            for s in range(4):
                load_gates(s, s)
                load_hid(s, s)
            with sp.Fori(1, EARLY // 4) as r:
                for s in range(4):
                    sp.wait_ge(up_low, r * 4 + (s - 3))
                    load_up(r * 4 + s, s)
                    sp.wait_ge(w_ready, r * 4 + (s - 3))
                    load_gates(r * 4 + s, s)
                    load_hid(r * 4 + s, s)
            with sp.Fori(EARLY // 4, NK // 4 - 1) as r:
                for s in range(4):
                    sp.wait_ge(up_low, r * 4 + (s - 3))
                    load_up(r * 4 + s, s)
                    sp.wait_ge(w_ready, r * 4 + (s - 3))
                    load_gates(r * 4 + s, s)
                    sp.wait_ge(low_ready, r * 4 + (FRONT + s + 1))
                    load_down(r * 4 + (s + 4), s)
            for s in range(4):
                sp.wait_ge(up_low, NK - 4 + (s - 3))
                load_up(NK - 4 + s, s)
                sp.wait_ge(w_ready, NK - 4 + (s - 3))
                load_gates(NK - 4 + s, s)
            for t in range(NT):
                sp.wait_ge(fin_y, t + 1)
                sp.dma_start(out[t * P:(t + 1) * P, :], hn[:, t, :]).then_inc(out_stored, 16)
            sp.wait_ge(out_stored, 16 * NT)

        @block.gpsimd
        def _(pool):
            step = Steps(pool, pool_step)
            nc.gpsimd.memset(ones, 1.0).then_inc(consts, 1)
            step(nc.gpsimd.memset(ident, 0.0))
            nc.gpsimd.affine_select(out=ident, in_=ident, compare_op=ALU.not_equal, fill=1.0, base=0,
                                    pattern=[[-1, P]], channel_multiplier=1).then_inc(consts, 1)
            step(nc.gpsimd.memset(causal, 1.0))
            step(nc.gpsimd.affine_select(out=causal, in_=causal, compare_op=ALU.is_ge, fill=0.0, base=0,
                                         pattern=[[1, P]], channel_multiplier=-1))
            nc.gpsimd.affine_select(out=causal[:, CH:P], in_=causal[:, CH:P], compare_op=ALU.is_ge, fill=0.0,
                                    base=-CH, pattern=[[0, P - CH]], channel_multiplier=1).then_inc(consts, 1)
            nc.gpsimd.iota(iota, pattern=[[1, P]], base=0, channel_multiplier=0,
                           allow_small_or_imprecise_dtypes=True).then_inc(consts, 1)
            step(nc.gpsimd.memset(reset, 1.0))
            nc.gpsimd.memset(reset.rearrange("p (c t) -> p c t", t=CH)[:, :, 0:1], 0.0).then_inc(consts, 1)

            def low(b, s):
                pool.wait_ge(high_ready, b + 1)
                nc.gpsimd.tensor_tensor(w_half[1][:, s % 2, :], ring[:, s, :], w_half[0][:, s % 2, :].bitcast(F32),
                                        ALU.subtract).then_inc(low_ready, 1)

            def low_up(i, s):
                pool.wait_ge(up_high, i + 1)
                nc.gpsimd.tensor_tensor(up_half[1][:, s, :], uraw[:, s, :], up_half[0][:, s, :].bitcast(F32),
                                        ALU.subtract).then_inc(up_low, 1)

            with pool.Fori(0, (FRONT + EARLY) // 4) as r:
                for s in range(4):
                    low(r * 4 + s, s)
            for s in range(2):
                low(FRONT + EARLY + s, s)
            with pool.Fori(0, EARLY // 4) as r:
                for s in range(4):
                    low_up(r * 4 + s, s)

            def both(i0, slot):
                for k in range(2):
                    low(i0 + (FRONT + 2 + k), (FRONT + slot + 2 + k) % 4)
                for k in range(2):
                    low_up(i0 + k, (slot + k) % 4)

            both(EARLY, 0)
            with pool.Fori(0, (NK - EARLY) // 4 - 1) as r:
                both(r * 4 + (EARLY + 2), 2)
                both(r * 4 + (EARLY + 4), 0)
            for k in range(2):
                low_up(NK - 2 + k, 2 + k)

        @block.scalar
        def _(act):
            act.dma_start(x, x_in.rearrange("(t p) d -> p t d", p=P)).then_inc(ld_x, 16)
            act.dma_start(vec, vecs_in).then_inc(ld_vec, 16)
            act.dma_start(mem, mem_in.rearrange("(t p) d -> p t d", p=P)).then_inc(ld_mem, 16)
            act.dma_start(fin_w, final_in.to_broadcast([P, D])).then_inc(ld_fin, 16)
            act.sem_inc(bank_free, 4)
            act.sem_inc(gelu_out, 2)
            act.sem_inc(gate_out, 2)

            def norm(u, col):
                for t in range(u.tiles):
                    nc.scalar.activation(junk, u.src[:, t, :], ACT.Square, accum_out=ss[:, col + t:col + t + 1])\
                        .then_inc(u.sumsq, 1)
                    act.wait_ge(u.sumsq, t + 1)
                act.wait_ge(u.mean, 1)
                nc.scalar.activation(rt[:, col:col + u.tiles], ms[:, col:col + u.tiles], ACT.Sqrt).then_inc(u.root, 1)

            def high(b, s, landed):
                act.wait_ge(wt[s], landed)
                nc.scalar.activation(w_half[0][:, s % 2, :], ring[:, s, :], ACT.Copy).then_inc(high_ready, 1)

            def high_up(i, s, landed):
                act.wait_ge(ld_up[s], landed)
                nc.scalar.activation(up_half[0][:, s, :], uraw[:, s, :], ACT.Copy).then_inc(up_high, 1)

            def ahead(b):
                act.wait_ge(block_used, b + 1)
                high(b + 2, (b + 2) % 4, 16 * ((b + 2) // 4 + 1))

            act.wait_ge(ld_x, 16)
            norm(mixn, 0)
            high(0, 0, 16)
            high(1, 1, 16)
            act.wait_ge(ld_mem, 16)
            norm(memn, 4)
            act.wait_ge(lb_diff, 1)
            nc.scalar.activation(lbm[:, 4:12], lbm[:, 4:12], ACT.Exp).then_inc(lb_exp, 1)
            with act.Fori(0, 6) as r:
                for s in range(4):
                    act.wait_ge(block_used, r * 4 + (s + 1))
                    high(None, (s + 2) % 4, r * 16 + 16 * ((s + 2) // 4 + 1))
                    nc.scalar.activation(proj[:, bass.ds(r * 4 + s, 1), :], psum[:, s:s + 1, :], ACT.Copy)\
                        .then_inc(bank_free, 1)
            act.wait_ge(bank_free, 28)
            act.wait_ge(mixn.tr, KC)
            for n, (a, b) in enumerate(((pF, pF), (G, pQ), (kk, pG))):
                ahead(24 + n)
                nc.scalar.activation(a, b, ACT.Exp, scale=-1.0).then_inc(exp_fqg, 1)
            ahead(27)
            act.wait_ge(i_done, 1)
            for t in range(NT):
                nc.scalar.activation(iN[:, t, :], psum[:, 4 + t, :], ACT.Copy).then_inc(i_out, 1)
            act.wait_ge(fg_ready, 1)
            nc.scalar.activation(pF, pF, ACT.Ln).then_inc(logf_ready, 1)
            for b in range(KC):
                ahead(28 + b)
                nc.scalar.activation(KT[:, b, :], psum[:, b % 4, 0:NM], ACT.Copy).then_inc(k_out, 1)
                if b == 5:
                    act.wait_ge(G_ready, 1)
                    nc.scalar.activation(pF, G, ACT.Exp).then_inc(expG_ready, 1)
                if b == 6:
                    nc.scalar.activation(expN, G, ACT.Exp, scale=-1.0).then_inc(expG_ready, 1)
                if b == 7:
                    act.wait_ge(G_ready, 2)
                    nc.scalar.activation(expD, expD, ACT.Exp).then_inc(expG_ready, 1)
            for hf in range(2):
                for b in range(4):
                    ahead(36 + 4 * hf + b)
                act.wait_ge(v_done, hf + 1)
                for t in range(MT):
                    nc.scalar.activation(Vm[:, t, hf * 512:(hf + 1) * 512], psum[:, 4 + 2 * hf + t, :], ACT.Copy)\
                        .then_inc(v_out, 1)
            act.wait_ge(conv_sum, 1)
            nc.scalar.activation(junk[:, 0:SEQ], psum[:, 4, :], ACT.Copy, scale=1.0 / CW, bias=EPS).then_inc(act_step, 1)
            act.wait_ge(act_step, 1)
            nc.scalar.activation(junk[:, SEQ:2 * SEQ], junk[:, 0:SEQ], ACT.Sqrt).then_inc(conv_root, 1)
            for h in range(HH):
                act.wait_ge(ke_tr, h + 1)
                act.wait_ge(conv_y, 1)
                nc.scalar.activation(keN[:, h, :], psum[:, h, :], ACT.Copy).then_inc(ke_out, 1)
            for h in range(HH):
                act.wait_ge(o_done, h + 1)
                nc.scalar.activation(sq[:, h, :], psum[:, 4 + h, :], ACT.Square).then_inc(o_sq, 1)
            for h in range(HH):
                act.wait_ge(o_sum, h + 1)
                nc.scalar.activation(rinv[:, h, :], psum[:, h, :], ACT.Copy, scale=1.0 / P, bias=EPS)\
                    .then_inc(act_step, 1)
                act.wait_ge(act_step, 2 + h)
                nc.scalar.activation(rinv[:, h, :], rinv[:, h, :], ACT.Sqrt).then_inc(o_root, 1)
            for b in range(44, 52):
                ahead(b)
            act.wait_ge(x_mixed, 8)
            norm(attn, 0)
            for b in range(KC):
                ahead(52 + b)
                nc.scalar.activation(qT[:, b, :], psum[:, b % 4, :], ACT.Copy).then_inc(q_out, 1)
            for h in range(MH):
                act.wait_ge(sc_max, h + 1)
                for t in range(NT):
                    bank = 2 * (h % 2) + t // 2
                    nc.scalar.activation(prob[:, h % 2, t, :], psum[:, bank, (t % 2) * NM:(t % 2 + 1) * NM], ACT.Exp,
                                         scale=DH ** -0.5, bias=nmx[:, 4 * (h % 2) + t:4 * (h % 2) + t + 1],
                                         accum_out=den[:, 4 * (h % 2) + t:4 * (h % 2) + t + 1]).then_inc(sc_exp, 1)
                for m in range(MT):
                    act.wait_ge(p_tr, MT * h + m + 1)
                    nc.scalar.activation(pT[:, h % 2, m, :], psum[:, 4 + m, :], ACT.Copy).then_inc(pT_out, 1)
                for c in range(2):
                    act.wait_ge(ao_done, 2 * h + c + 1)
                    nc.scalar.activation(hT_half[0][:, 2 * h + c, :], psum[:, 6 + c, :], ACT.Copy).then_inc(ao_high, 1)
            act.dma_start(keysT, keys_in).then_inc(ld_keys, 16)
            for b in range(60, 68):
                ahead(b)
            act.wait_ge(x_att, 8)
            norm(ffnn, 0)
            with act.Fori(0, 4) as r:
                for s in range(4):
                    act.wait_ge(block_used, r * 4 + (68 + s + 1))
                    high(None, (s + 2) % 4, r * 16 + 16 * ((68 + s + 2) // 4 + 1))
                    nc.scalar.activation(qpT[:, bass.ds(r * 4 + s, 1), :], psum[:, s:s + 1, :], ACT.Copy)\
                        .then_inc(qp_out, 1)
            for b in range(16):
                act.wait_ge(pk_done, b + 1)
                nc.scalar.activation(score[:, b // 4, (b % 4) * 512:(b % 4 + 1) * 512], psum[:, 4 + b % 4, :], ACT.Copy)\
                    .then_inc(pk_out, 1)
            def early(i, s, landed, used, slot_free, done):
                act.wait_ge(block_used, used)
                high(None, (s + 2) % 4, landed)
                if slot_free is not None:
                    act.wait_ge(hid_stored[s % 2], slot_free)
                nc.scalar.activation(hid[s % 2], psum[:, 4 + s % 2, :], ACT.Gelu).then_inc(gelu_out, 1)
                act.wait_ge(gelu_out, done)
                act.dma_start(hid_dram[bass.ds(i, 1)].rearrange("b p n -> (b p) n"), hid[s % 2])\
                    .then_inc(hid_stored[s % 2], 16)

            def early_at(i):
                early(i, i % 4, 16 * ((FRONT + i + 2) // 4 + 1), FRONT + i + 1, 16 * (i // 2) if i > 1 else None, i + 3)

            for t in range(NT):
                if t == 0:
                    for i in range(AHEAD):
                        early_at(i)
                else:
                    with act.Fori(t * AHEAD // 4, (t + 1) * AHEAD // 4) as r:
                        for s in range(4):
                            early(r * 4 + s, s, r * 16 + 16 * ((FRONT + s + 2) // 4 + 1), r * 4 + (FRONT + s + 1),
                                  r * 32 + 16 * (s // 2), r * 4 + (s + 3))
                act.wait_ge(best_ready, t + 1)
                nc.scalar.activation(ebest, ebest, ACT.Exp).then_inc(e_ready, 1)
                act.wait_ge(hk_tr, t + 1)
                nc.scalar.activation(hkT[:, :, t * P:(t + 1) * P],
                                     psum[:, 6, 0:3 * P].rearrange("p (a b) -> p a b", a=3), ACT.Copy)\
                    .then_inc(hkT_out, 1)
            for c in range(NCH):
                if c >= 2:
                    act.wait_ge(stored[c % 2], 16 * (c // 2))
                for k in range(CH // TB):
                    n = c * (CH // TB) + k
                    act.wait_ge(gate_done, n + 1)
                    nc.scalar.activation(
                        stage[:, c % 2, :, k * TB:(k + 1) * TB].rearrange("p i n -> p n i"),
                        psum[:, 2 * (n % 2):2 * (n % 2) + 2, :].rearrange("p b (n i) -> p (b n) i", i=P), ACT.Copy)\
                        .then_inc(gate_out, 1)
                act.wait_ge(gate_out, (c + 1) * (CH // TB) + 2)
                act.dma_start(gate_dram[:, :, c * CH:(c + 1) * CH], stage[:, c % 2]).then_inc(stored[c % 2], 16)
                early_at(4 * AHEAD + c)
            for s in range(2):
                act.wait_ge(stored[s], 16 * NT)
            for i in range(4):
                high_up(i, i, 16)
            with act.Fori(1, EARLY // 4) as r:
                for s in range(4):
                    if s % 2 == 0:
                        act.wait_ge(up_done, r * 16 + (8 * (s // 2) - 8))
                    high_up(None, s, r * 16 + 16)

            def both(i0, slot, landed, used, up_free, last=False):
                for k in range(2):
                    act.wait_ge(block_used, used + k)
                    if not last:
                        high(None, (slot + 2 + k) % 4, landed)
                    act.wait_ge(w_ready, i0 + (k - 1))
                    nc.scalar.activation(hid[k], psum[:, 4 + k, :], ACT.Gelu).then_inc(gelu_out, 1)
                act.wait_ge(up_done, up_free)
                for k in range(2):
                    high_up(None, slot + k, landed - 16 * ((slot + 2) // 4) - 16 * (FRONT // 4))

            for s in range(2):
                act.wait_ge(hid_stored[s], 16 * EARLY // 2)
            both(EARLY, 0, 16 * ((FRONT + EARLY + 2) // 4 + 1), FRONT + EARLY + 1, 4 * EARLY - 8)
            with act.Fori(EARLY // 4, NK // 4 - 1) as r:
                both(r * 4 + 2, 2, r * 16 + (16 * (FRONT // 4) + 32), r * 4 + (FRONT + 3), r * 16)
                both(r * 4 + 4, 0, r * 16 + (16 * (FRONT // 4) + 32), r * 4 + (FRONT + 5), r * 16 + 8)
            both(NK - 2, 2, 16 * (NK // 4 + FRONT // 4) + 16, FRONT + NK - 1, 4 * NK - 16, last=True)
            act.wait_ge(x_added, 8 * GROUPS + 4)
            for t in range(NT):
                nc.scalar.activation(junk, x[:, t, :], ACT.Square, accum_out=ss[:, t:t + 1]).then_inc(fin_sq, 1)
                act.wait_ge(fin_sq, t + 1)
            act.wait_ge(fin_mean, 1)
            nc.scalar.activation(rt[:, 0:NT], ms[:, 0:NT], ACT.Sqrt).then_inc(fin_root, 1)

        @block.vector
        def _(dve):
            step = Steps(dve, dve_step)
            dve.sem_inc(x_added, 4)

            def norm_rows(u, col):
                dve.wait_ge(u.sumsq, u.tiles)
                nc.vector.tensor_scalar(ms[:, col:col + u.tiles], ss[:, col:col + u.tiles], 1.0 / D, EPS,
                                        ALU.mult, ALU.add).then_inc(u.mean, 1)
                dve.wait_ge(u.root, 1)
                step(nc.vector.reciprocal(rs[:, col:col + u.tiles], rt[:, col:col + u.tiles]))
                for t in range(u.tiles):
                    nc.vector.tensor_scalar(u.dst[:, t, :], u.src[:, t, :], rs[:, col + t:col + t + 1], None, ALU.mult)\
                        .then_inc(u.h, 1)

            def norm_gain(u):
                for k in range(KC):
                    dve.wait_ge(u.tr, k + 1)
                    gain, cols = vec[:, u.gain + k:u.gain + k + 1], psum[:, 4 + k % 4, 0:u.tiles * P]
                    step(nc.vector.tensor_scalar(u.hT[0][:, k, :], cols, gain, None, ALU.mult))
                    nc.vector.scalar_tensor_tensor(u.hT[1][:, k, :], cols, gain, u.hT[0][:, k, :].bitcast(F32),
                                                   ALU.mult, ALU.subtract).then_inc(u.ready, 1)

            dve.wait_ge(ld_vec, 16)
            norm_rows(mixn, 0)
            norm_gain(mixn)
            norm_rows(memn, 4)
            l0, l1 = vec[:, V_LB0:V_LB0 + HH], vec[:, V_LB1:V_LB1 + HH]
            step(nc.vector.tensor_tensor(lbm[:, 0:4], l0, l1, ALU.max))
            step(nc.vector.tensor_tensor(lbm[:, 4:8], l0, lbm[:, 0:4], ALU.subtract))
            nc.vector.tensor_tensor(lbm[:, 8:12], l1, lbm[:, 0:4], ALU.subtract).then_inc(lb_diff, 1)
            dve.wait_ge(lb_exp, 1)
            step(nc.vector.tensor_tensor(lbm[:, 12:16], lbm[:, 4:8], lbm[:, 8:12], ALU.add))
            step(nc.vector.reciprocal(lbm[:, 16:20], lbm[:, 12:16]))
            step(nc.vector.tensor_tensor(lb, lbm[:, 4:8], lbm[:, 16:20], ALU.mult))
            step(nc.vector.tensor_scalar(oml, lb, -1.0, 1.0, ALU.mult, ALU.add))
            for n, (e, a) in enumerate(((G, pQ), (kk, pG))):
                dve.wait_ge(exp_fqg, n + 2)
                step(nc.vector.tensor_scalar(e, e, 1.0, None, ALU.add))
                step(nc.vector.reciprocal(e, e))
                step(nc.vector.tensor_tensor(a, a, e, ALU.mult))
            step(nc.vector.tensor_scalar(pF, pF, 1.0, None, ALU.add))
            step(nc.vector.reciprocal(pF, pF))
            for h in range(HH):
                step(nc.vector.tensor_scalar(pF[:, h, :], pF[:, h, :], oml[:, h:h + 1], lb[:, h:h + 1],
                                             ALU.mult, ALU.add))
            nc.vector.tensor_scalar(kk, pF, -1.0, 1.0, ALU.mult, ALU.add).then_inc(fg_ready, 1)
            norm_gain(memn)
            dve.wait_ge(consts, 5)
            dve.wait_ge(logf_ready, 1)
            for h in range(HH):
                step(nc.vector.tensor_tensor_scan(G[:, h, :], reset, pF[:, h, :], 0.0, ALU.mult, ALU.add))
            dve.wait_ge(i_done, 1)
            nc.vector.tensor_copy(rs[:, 15:16], G[:, 0, 0:1]).then_inc(G_ready, 1)
            Gc = G.rearrange("p h (c t) -> p (h c) t", t=CH)
            nc.vector.tensor_tensor(expD.rearrange("p h (c t) -> p (h c) t", t=CH),
                                    Gc[:, :, CH - 1:CH].to_broadcast([P, HH * NCH, CH]), Gc, ALU.subtract)\
                .then_inc(G_ready, 1)
            dve.wait_ge(expG_ready, 1)
            step(nc.vector.tensor_copy(decay, pF.rearrange("p h (c t) -> p h c t", t=CH)[:, :, :, CH - 1]))
            step(nc.vector.tensor_tensor(pQ, pQ, pF, ALU.mult))
            dve.wait_ge(expG_ready, 3)
            step(nc.vector.tensor_tensor(expN, kk, expN, ALU.mult))
            nc.vector.tensor_tensor(expD, kk, expD, ALU.mult).then_inc(qk_ready, 1)
            for c in range(CC):
                cw = [vec[:, V_CW + CC * j + c:V_CW + CC * j + c + 1] for j in range(3)]
                y, u = pV[:, c, :], pC[:, c, :]
                step(nc.vector.tensor_tensor(u, u, pV[:, c, :], ALU.mult))
                step(nc.vector.tensor_scalar(y, u, cw[2], None, ALU.mult))
                step(nc.vector.scalar_tensor_tensor(y[:, 1:], u[:, :SEQ - 1], cw[1], y[:, 1:], ALU.mult, ALU.add))
                step(nc.vector.scalar_tensor_tensor(y[:, 2:], u[:, :SEQ - 2], cw[0], y[:, 2:], ALU.mult, ALU.add))
                step(nc.vector.tensor_tensor(y, y, pB[:, c, :], ALU.mult))
                nc.vector.tensor_tensor(csq[:, c, :], y, y, ALU.mult).then_inc(conv_sq, 1)
            dve.wait_ge(conv_root, 1)
            step(nc.vector.reciprocal(junk[:, 0:SEQ], junk[:, SEQ:2 * SEQ]))
            for c in range(CC):
                step.put(nc.vector.scalar_tensor_tensor(pB[:, c, :], pV[:, c, :], vec[:, V_CONV + c:V_CONV + c + 1],
                                                        junk[:, 0:SEQ], ALU.mult, ALU.mult))
            step.end()
            nc.vector.tensor_copy(rs[:, 14:15], rs[:, 15:16]).then_inc(conv_y, 1)
            step(nc.vector.memset(aT, 0.0))
            for h in range(HH):
                dve.wait_ge(a_done, h + 1)
                nc.vector.copy_predicated(
                    aT[:, h, :].rearrange("p (t c) -> p t c", c=P),
                    causal.bitcast(U32).rearrange("p (a c) -> p a c", a=1).to_broadcast([P, NT, P]),
                    psum[:, 4 + h, :].rearrange("p (t c) -> p t c", c=P)).then_inc(a_ready, 1)
            for h in range(HH):
                dve.wait_ge(u_done, h + 1)
                for n in range(NCH - 1):
                    u = psum[:, 2 * (h % 2) + n % 2, (n // 2) * P:(n // 2 + 1) * P]
                    if n == 0:
                        ins = nc.vector.tensor_copy(S[:, h, 1, :], u)
                    else:
                        ins = nc.vector.scalar_tensor_tensor(S[:, h, n + 1, :], S[:, h, n, :], decay[:, h, n:n + 1], u,
                                                             ALU.mult, ALU.add)
                    ins.then_inc(s_ready, 1)
                    dve.wait_ge(s_ready, h * (NCH - 1) + n + 1)
            for h in range(HH):
                dve.wait_ge(o_root, h + 1)
                step(nc.vector.reciprocal(rinv[:, h, :], rinv[:, h, :]))
                step(nc.vector.scalar_tensor_tensor(rinv[:, h, :], rinv[:, h, :], vec[:, V_HGRN + h:V_HGRN + h + 1],
                                                    pG[:, h, :], ALU.mult, ALU.mult))
                step.put(nc.vector.tensor_tensor(rinv[:, h, :], rinv[:, h, :], psum[:, 4 + h, :], ALU.mult))
            step.end()
            for c in range(KC):
                y = pB[:, c, :] if c < CC else rinv[:, c - CC, :]
                step(nc.vector.tensor_copy(hT_half[0][:, c, :], y))
                nc.vector.tensor_tensor(hT_half[1][:, c, :], y, hT_half[0][:, c, :].bitcast(F32), ALU.subtract)\
                    .then_inc(y_ready, 1)

            def residual(done, added):
                for hf in range(2):
                    dve.wait_ge(done, hf + 1)
                    for t in range(NT):
                        nc.vector.tensor_tensor(x[:, t, hf * 512:(hf + 1) * 512], x[:, t, hf * 512:(hf + 1) * 512],
                                                psum[:, 4 * hf + t, :], ALU.add).then_inc(added, 1)

            residual(mix_done, x_mixed)
            dve.wait_ge(x_mixed, 8)
            norm_rows(attn, 0)
            norm_gain(attn)
            for h in range(MH):
                o = 4 * (h % 2)
                dve.wait_ge(sc_done, h + 1)
                step(nc.vector.tensor_reduce(mx[:, o:o + NT].rearrange("p (a b) -> p a b", a=2),
                                             psum[:, 2 * (h % 2):2 * (h % 2) + 2, :].rearrange("p a (b m) -> p a b m", b=2),
                                             AX_X, ALU.max))
                nc.vector.tensor_scalar(nmx[:, o:o + NT], mx[:, o:o + NT], -DH ** -0.5, None, ALU.mult).then_inc(sc_max, 1)
                dve.wait_ge(sc_exp, NT * (h + 1))
                step(nc.vector.reciprocal(rden[:, o:o + NT], den[:, o:o + NT]))
                for t in range(NT):
                    nc.vector.tensor_scalar(prob[:, h % 2, t, :], prob[:, h % 2, t, :], rden[:, o + t:o + t + 1], None,
                                            ALU.mult).then_inc(p_ready, 1)
                for c in range(2):
                    dve.wait_ge(ao_high, 2 * h + c + 1)
                    nc.vector.tensor_tensor(hT_half[1][:, 2 * h + c, :], psum[:, 6 + c, :],
                                            hT_half[0][:, 2 * h + c, :].bitcast(F32), ALU.subtract).then_inc(ao_out, 1)
            residual(att_done, x_att)
            dve.wait_ge(x_att, 8)
            norm_rows(ffnn, 0)
            norm_gain(ffnn)

            def top16(lists):
                for values, vals, index in lists:
                    step.put(nc.vector.max(vals[:, 0:8], values))
                step.end()
                for values, vals, index in lists:
                    step.put(nc.vector.max_index(index[:, 0:8], vals[:, 0:8], values))
                    step.put(nc.vector.match_replace(values, vals[:, 0:8], values, NEG))
                step.end()
                for values, vals, index in lists:
                    step.put(nc.vector.max(vals[:, 8:16], values))
                step.end()
                for values, vals, index in lists:
                    step.put(nc.vector.max_index(index[:, 8:16], vals[:, 8:16], values))
                step.end()

            dve.wait_ge(pk_out, 16)
            for t in range(NT):
                top16([(score[:, t, j * NK:(j + 1) * NK], top[:, j, :], topi[:, j, :].bitcast(U32)) for j in range(16)])
                step(nc.vector.tensor_copy(topf, topi.bitcast(U32)))
                half = top.rearrange("p (h q) k -> p h q k", q=2)
                step(nc.vector.tensor_tensor(
                    cand.rearrange("p h (a b) -> p h a b", a=TK),
                    half[:, :, 0, :].rearrange("p h (a b) -> p h a b", b=1).to_broadcast([P, PH, TK, TK]),
                    half[:, :, 1, :].rearrange("p h (a b) -> p h a b", a=1).to_broadcast([P, PH, TK, TK]), ALU.add))
                top16([(cand[:, h, :], best[:, h, :], pos[:, h, :].bitcast(U32)) for h in range(PH)])
                nc.vector.tensor_tensor(ebest, best, best[:, :, 0:1].to_broadcast([P, PH, TK]), ALU.subtract)\
                    .then_inc(best_ready, 1)
                step(nc.vector.tensor_scalar(posd.bitcast(U32), pos.bitcast(U32), 4, None, ALU.logical_shift_right))
                step(nc.vector.tensor_copy(posf[:, 0], posd.bitcast(U32)))
                step(nc.vector.tensor_scalar(posd.bitcast(U32), pos.bitcast(U32), TK - 1, None, ALU.bitwise_and))
                step(nc.vector.tensor_copy(posf[:, 1], posd.bitcast(U32)))
                halff = topf.rearrange("p (h q) k -> p h q k", q=2)
                for q in range(2):
                    step(nc.vector.tensor_tensor(
                        onehot.rearrange("p h (k a) -> p (h k) a", a=TK),
                        posf[:, q].rearrange("p h (k b) -> p (h k) b", b=1).to_broadcast([P, PH * TK, TK]),
                        iota[:, 0:TK].rearrange("p (b a) -> p b a", b=1).to_broadcast([P, PH * TK, TK]), ALU.is_equal))
                    step(nc.vector.tensor_tensor(
                        onehot.rearrange("p h (k a) -> p h k a", a=TK),
                        onehot.rearrange("p h (k a) -> p h k a", a=TK),
                        halff[:, :, q, :].rearrange("p h (b a) -> p h b a", b=1).to_broadcast([P, PH, TK, TK]), ALU.mult))
                    step(nc.vector.tensor_reduce(hk[:, q, :], onehot.rearrange("p h (k a) -> p (h k) a", a=TK),
                                                 AX_X, ALU.add))
                dve.wait_ge(e_ready, t + 1)
                step(nc.vector.tensor_reduce(esum[:, 0:PH], ebest, AX_X, ALU.add))
                step(nc.vector.reciprocal(esum[:, 8:16], esum[:, 0:8]))
                nc.vector.tensor_tensor(hk[:, 2, :].rearrange("p (h k) -> p h k", k=TK), ebest,
                                        esum[:, 8:16].rearrange("p (h k) -> p h k", k=1).to_broadcast([P, PH, TK]),
                                        ALU.mult).then_inc(hk_ready, 1)
                dve.wait_ge(hkT_out, t + 1)

            def hots(n, s):
                for j in range(TB):
                    nc.vector.tensor_scalar(hot[:, s, 0, j * P:(j + 1) * P], iota, hkT[:, 0, bass.ds(n + j, 1)], None,
                                            ALU.is_equal)
                    ins = nc.vector.tensor_scalar(hot[:, s, 1, j * P:(j + 1) * P], iota, hkT[:, 1, bass.ds(n + j, 1)],
                                                  hkT[:, 2, bass.ds(n + j, 1)], ALU.is_equal, ALU.mult)
                ins.then_inc(hot_ready, 1)

            for s in range(2):
                hots(s * TB, s)
            with dve.Fori(1, SEQ // TB // 2) as r:
                for s in range(2):
                    dve.wait_ge(gate_done, r * 2 + (s - 1))
                    hots(r * (2 * TB) + s * TB, s)

            def weigh(i, s, landed, spilled):
                dve.wait_ge(ld_gate[s], landed)
                if spilled:
                    dve.wait_ge(ld_hid[s], landed)
                else:
                    dve.wait_ge(gelu_out, i + 3)
                w = wraw[:, s % 2, :]
                nc.vector.tensor_tensor(w, hidr[:, s, :] if spilled else hid[s % 2], gates[:, s, :], ALU.mult)\
                    .then_inc(w_raw, 1)
                dve.wait_ge(w_raw, i + 1)
                nc.vector.tensor_copy(wgt_half[0][:, s, :], w).then_inc(w_high, 1)
                dve.wait_ge(w_high, i + 1)
                nc.vector.tensor_tensor(wgt_half[1][:, s, :], w, wgt_half[0][:, s, :].bitcast(F32), ALU.subtract)\
                    .then_inc(w_ready, 1)

            def accumulate(g):
                for o in range(8):
                    dve.wait_ge(up_done, g * 8 + (o + 1))
                    xs = x[:, o // 2, (o % 2) * 512:(o % 2 + 1) * 512]
                    nc.vector.tensor_tensor(xs, xs, psum[:, o % 4, :], ALU.add).then_inc(x_added, 1)

            dve.wait_ge(gate_done, SEQ // TB)
            for i in range(4):
                weigh(i, i, 16, True)
            accumulate(0)
            with dve.Fori(1, EARLY // 4) as r:
                for q in range(2):
                    for s in (2 * q, 2 * q + 1):
                        weigh(r * 4 + s, s, r * 16 + 16, True)
                    accumulate(r * 2 + (q - 1))
            for i in (EARLY, EARLY + 1):
                weigh(i, i % 4, 4 * EARLY + 16, False)
            accumulate(FIRST_D)
            with dve.Fori(EARLY // 4, NK // 4 - 1) as r:
                for s in (2, 3):
                    weigh(r * 4 + s, s, r * 16 + 16, False)
                accumulate(r * 2)
                for s in (0, 1):
                    weigh(r * 4 + (s + 4), s, r * 16 + 32, False)
                accumulate(r * 2 + 1)
            for i in (NK - 2, NK - 1):
                weigh(i, i % 4, 4 * NK, False)
            accumulate(GROUPS - 2)
            accumulate(GROUPS - 1)
            dve.wait_ge(fin_sq, NT)
            nc.vector.tensor_scalar(ms[:, 0:NT], ss[:, 0:NT], 1.0 / D, EPS, ALU.mult, ALU.add).then_inc(fin_mean, 1)
            dve.wait_ge(fin_root, 1)
            step(nc.vector.reciprocal(rs[:, 0:NT], rt[:, 0:NT]))
            dve.wait_ge(ld_fin, 16)
            for t in range(NT):
                nc.vector.scalar_tensor_tensor(hn[:, t, :], x[:, t, :], rs[:, t:t + 1], fin_w, ALU.mult, ALU.mult)\
                    .then_inc(fin_y, 1)

        @block.tensor
        def _(pe):
            pe.wait_ge(consts, 5)

            def turn(u):
                pe.wait_ge(u.h, u.tiles)
                for k in range(KC):
                    if k >= 4:
                        pe.wait_ge(u.ready, k - 3)
                    for t in range(u.tiles):
                        ins = nc.tensor.transpose(psum[:, 4 + k % 4, t * P:(t + 1) * P], u.dst[:, t, k * P:(k + 1) * P], ident)
                    ins.then_inc(u.tr, 1)

            def three(out, lhs, rhs, first, last):
                nc.tensor.matmul(out, lhs[0], rhs[0], start=first, stop=False)
                nc.tensor.matmul(out, lhs[0], rhs[1], start=False, stop=False)
                return nc.tensor.matmul(out, lhs[1], rhs[0], start=False, stop=last)

            def columns(b, s, rhs, n, bank):
                pe.wait_ge(low_ready, b + 1)
                for k in range(KC):
                    ins = three(psum[:, bank, 0:n], [w[:, s % 2, k * P:(k + 1) * P] for w in w_half],
                                [r[:, k, :] for r in rhs], k == 0, k == KC - 1)
                ins.then_inc(block_used, 1)

            def rows(b, lhs, banks, k0):
                pe.wait_ge(low_ready, b + 1)
                for j in range(2):
                    for n, bank in enumerate(banks):
                        ins = three(psum[:, bank, :], [a[:, k0 + j, n * P:(n + 1) * P] for a in lhs],
                                    [w[:, b % 2, j * 512:(j + 1) * 512] for w in w_half],
                                    k0 + j == 0, k0 + j == KC - 1)
                ins.then_inc(block_used, 1)

            turn(mixn)
            pe.wait_ge(mixn.ready, KC)
            with pe.Fori(0, 6) as r:
                for s in range(4):
                    pe.wait_ge(bank_free, r * 4 + (s + 1))
                    columns(r * 4 + s, s, hT_half, SEQ, s)
            for s in range(4):
                rows(24 + s, hT_half, range(4, 8), 2 * s)
            pe.wait_ge(block_used, 28)
            pe.sem_inc(i_done, 1)
            pe.wait_ge(i_out, NT)
            turn(memn)
            pe.wait_ge(memn.ready, KC)
            pe.wait_ge(bank_free, 28)
            for b in range(KC):
                if b >= 4:
                    pe.wait_ge(k_out, b - 3)
                columns(28 + b, b, memT_half, NM, b % 4)
            for hf in range(2):
                for s in range(4):
                    rows(36 + 4 * hf + s, memT_half, range(4 + 2 * hf, 6 + 2 * hf), 2 * s)
                pe.wait_ge(block_used, 40 + 4 * hf)
                pe.sem_inc(v_done, 1)
            pe.wait_ge(v_out, 2 * MT)
            pe.wait_ge(conv_sq, CC)
            for c in range(CC):
                ins = nc.tensor.matmul(psum[:, 4, :], ones, csq[:, c, :], start=(c == 0), stop=(c == CC - 1))
            ins.then_inc(conv_sum, 1)
            pe.wait_ge(qk_ready, 1)
            pe.wait_ge(k_out, KC)
            for h in range(HH):
                for t in range(NT):
                    ins = nc.tensor.transpose(psum[:, h, t * P:(t + 1) * P], expD[:, h, t * P:(t + 1) * P], ident)
                ins.then_inc(ke_tr, 1)
            pe.wait_ge(conv_y, 1)
            for h in range(HH):
                for t in range(NT):
                    ins = nc.tensor.matmul(psum[:, 4 + h, t * P:(t + 1) * P], expN[:, h, t * P:(t + 1) * P],
                                           pQ[:, h, t * P:(t + 1) * P], start=True, stop=True)
                ins.then_inc(a_done, 1)
            for h in range(HH):
                pe.wait_ge(ke_out, HH)
                if h >= 2:
                    pe.wait_ge(s_ready, (h - 1) * (NCH - 1))
                for n in range(NCH - 1):
                    lo = (n % 2) * CH
                    ins = nc.tensor.matmul(psum[:, 2 * (h % 2) + n % 2, (n // 2) * P:(n // 2 + 1) * P],
                                           keN[lo:lo + CH, h, (n // 2) * P:(n // 2 + 1) * P],
                                           iN[lo:lo + CH, n // 2, h * P:(h + 1) * P], start=True, stop=True)
                ins.then_inc(u_done, 1)
            for h in range(HH):
                pe.wait_ge(a_ready, h + 1)
                pe.wait_ge(s_ready, (h + 1) * (NCH - 1))
                for t in range(NT):
                    nc.tensor.matmul(psum[:, 4 + h, t * P:(t + 1) * P], iN[:, t, h * P:(h + 1) * P],
                                     aT[:, h, t * P:(t + 1) * P], start=True, stop=False, skip_group_check=True)
                    for n in (2 * t, 2 * t + 1):
                        if n == 0:
                            continue
                        ins = nc.tensor.matmul(psum[:, 4 + h, n * CH:(n + 1) * CH], S[:, h, n, :],
                                               pQ[:, h, n * CH:(n + 1) * CH], start=False, stop=(n % 2 == 1),
                                               skip_group_check=True)
                ins.then_inc(o_done, 1)
            for h in range(HH):
                pe.wait_ge(o_sq, h + 1)
                nc.tensor.matmul(psum[:, h, :], ones, sq[:, h, :], start=True, stop=True).then_inc(o_sum, 1)

            def product(lhs, b0, done, first):
                for hf in range(2):
                    pe.wait_ge(*first[hf])
                    for s in range(4):
                        rows(b0 + 4 * hf + s, lhs, range(4 * hf, 4 * hf + 4), 2 * s)
                    pe.wait_ge(block_used, b0 + 4 * hf + 4)
                    pe.sem_inc(done, 1)

            product(hT_half, 44, mix_done, ((y_ready, KC), (y_ready, KC)))
            turn(attn)
            pe.wait_ge(attn.ready, KC)
            for b in range(KC):
                if b >= 4:
                    pe.wait_ge(q_out, b - 3)
                columns(52 + b, b, hT_half, SEQ, b % 4)
            pe.wait_ge(q_out, KC)
            for h in range(MH):
                if h >= 2:
                    pe.wait_ge(sc_exp, NT * (h - 1))
                for t in range(NT):
                    for c in range(2):
                        ins = nc.tensor.matmul(psum[:, 2 * (h % 2) + t // 2, (t % 2) * NM:(t % 2 + 1) * NM],
                                               qT[:, 2 * h + c, t * P:(t + 1) * P], KT[:, 2 * h + c, :],
                                               start=(c == 0), stop=(c == 1), skip_group_check=True)
                ins.then_inc(sc_done, 1)
                pe.wait_ge(p_ready, NT * (h + 1))
                for m in range(MT):
                    if h:
                        pe.wait_ge(pT_out, MT * (h - 1) + m + 1)
                    for t in range(NT):
                        ins = nc.tensor.transpose(psum[:, 4 + m, t * P:(t + 1) * P], prob[:, h % 2, t, m * P:(m + 1) * P], ident)
                    ins.then_inc(p_tr, 1)
                pe.wait_ge(pT_out, MT * (h + 1))
                for c in range(2):
                    if h:
                        pe.wait_ge(ao_out, 2 * (h - 1) + c + 1)
                    for m in range(MT):
                        ins = nc.tensor.matmul(psum[:, 6 + c, :], Vm[:, m, h * DH + c * P:h * DH + (c + 1) * P],
                                               pT[:, h % 2, m, :], start=(m == 0), stop=(m == MT - 1))
                    ins.then_inc(ao_done, 1)
            pe.wait_ge(ao_out, 2 * MH)
            product(hT_half, 60, att_done, ((sc_exp, NT * MH), (ao_out, 2 * MH)))
            turn(ffnn)
            pe.wait_ge(ffnn.ready, KC)
            for s in range(4):
                columns(68 + s, s, hT_half, SEQ, s)
            with pe.Fori(1, 4) as r:
                for s in range(4):
                    pe.wait_ge(qp_out, r * 4 + (s - 3))
                    columns(r * 4 + (68 + s), s, hT_half, SEQ, s)
            pe.wait_ge(ld_keys, 16)
            pe.wait_ge(qp_out, 16)
            for b in range(16):
                if b >= 4:
                    pe.wait_ge(pk_out, b - 3)
                for j in range(4):
                    hp = 4 * (b % 4) + j
                    ins = nc.tensor.matmul(psum[:, 4 + b % 4, j * NK:(j + 1) * NK], qpT[:, hp, (b // 4) * P:(b // 4 + 1) * P],
                                           keysT[:, hp, :], start=True, stop=True)
                ins.then_inc(pk_done, 1)

            def first_product(i, s):
                pe.wait_ge(gelu_out, i + 1)
                columns(i + FRONT, s, hT_half, SEQ, 4 + s % 2)

            def gate_step(n, s):
                pe.wait_ge(hot_ready, n + 1)
                pe.wait_ge(gate_out, n + 1)
                for j in range(TB):
                    ins = nc.tensor.matmul(psum[:, 2 * s + j // 4, (j % 4) * P:(j % 4 + 1) * P],
                                           hot[:, s, 1, j * P:(j + 1) * P], hot[:, s, 0, j * P:(j + 1) * P],
                                           start=True, stop=True)
                ins.then_inc(gate_done, 1)

            def second_product(g, s):
                pe.wait_ge(up_low, g * GT + GT)
                pe.wait_ge(w_ready, g * GT + GT)
                for o in range(8):
                    pe.wait_ge(x_added, g * 8 + (o + 1))
                    for t in range(GT):
                        ins = three(psum[:, o % 4, :], [w[:, s + t, (o // 2) * P:(o // 2 + 1) * P] for w in wgt_half],
                                    [u[:, s + t, (o % 2) * 512:(o % 2 + 1) * 512] for u in up_half],
                                    t == 0, t == GT - 1)
                    ins.then_inc(up_done, 1)

            pe.wait_ge(pk_out, 16)
            for t in range(NT):
                with pe.Fori(t * AHEAD // 4, (t + 1) * AHEAD // 4) as r:
                    for s in range(4):
                        first_product(r * 4 + s, s)
                pe.wait_ge(hk_ready, t + 1)
                for j in range(3):
                    ins = nc.tensor.transpose(psum[:, 6, j * P:(j + 1) * P], hk[:, j, :], ident)
                ins.then_inc(hk_tr, 1)
            with pe.Fori(0, 2) as r:
                for c in range(4):
                    with pe.Fori(0, CH // TB // 2) as k:
                        for s in range(2):
                            gate_step(r * (NCH // 2 * CH // TB) + k * 2 + (c * (CH // TB) + s), s)
                    first_product(r * 4 + (4 * AHEAD + c), c)
            pe.wait_ge(gate_out, SEQ // TB + 2)
            second_product(0, 0)
            with pe.Fori(0, (FIRST_D - 1) // 2) as r:
                second_product(r * 2 + 1, 2)
                second_product(r * 2 + 2, 0)
            first_product(EARLY, 0)
            first_product(EARLY + 1, 1)
            second_product(FIRST_D, 2)
            with pe.Fori(EARLY // 4, NK // 4 - 1) as r:
                first_product(r * 4 + 2, 2)
                first_product(r * 4 + 3, 3)
                second_product(r * 2, 0)
                first_product(r * 4 + 4, 0)
                first_product(r * 4 + 5, 1)
                second_product(r * 2 + 1, 2)
            first_product(NK - 2, 2)
            first_product(NK - 1, 3)
            second_product(GROUPS - 2, 0)
            second_product(GROUPS - 1, 2)


def kernel(**inputs):
    import numpy as np
    import concourse.bacc as bacc
    from concourse.bass_utils import run_bass_kernel_spmd

    def cols(w):
        return w.reshape(KC, P, -1, P).transpose(2, 1, 0, 3).reshape(-1, P, D)

    def rws(w):
        return w.reshape(4, 2, P, -1, 512).transpose(3, 0, 2, 1, 4).reshape(-1, P, D)

    def vec(v):
        return v.reshape(-1, P).T

    i = {k: np.asarray(v) for k, v in inputs.items()}
    w_in, wkv = i["w_in"][0], i["wkv_mem"][0]
    o0 = 3 * CW
    front = np.ascontiguousarray(np.concatenate([
        cols(w_in[:, :o0 + 2 * CW]), cols(w_in[:, o0 + 3 * CW:]), rws(w_in[:, o0 + 2 * CW:o0 + 3 * CW]),
        cols(wkv[:, :D]), rws(wkv[:, D:]), rws(i["w_out"][0]), cols(i["wq_mem"][0]), rws(i["wo_mem"][0]),
        cols(i["peer_w_query"][0])]))
    vecs = np.ascontiguousarray(np.concatenate([
        vec(i["mix_norm_w"][0]), vec(i["conv_norm_w"][0]), vec(i["hgrn_norm_w"][0]), vec(i["hgrn_lb_logits"][0]),
        vec(i["hgrn_lb_logits"][1]), vec(i["xattn_norm_w"][0]), vec(i["mem_norm_w"][0]), vec(i["ffn_norm_w"][0]),
        vec(i["conv_w"][0].reshape(-1))], axis=1))
    down = i["peer_down"][0].reshape(NK, P, KC, P).transpose(0, 3, 2, 1).reshape(NK, P, D)
    arrays = {
        "x_in": i["x"][0], "mem_in": i["mem"][0], "vecs_in": vecs, "final_in": i["final_norm_w"].reshape(1, D),
        "front_w": front, "keys_in": i["peer_sub_keys"][0].reshape(16, NK, P).transpose(2, 0, 1),
        "down_in": down, "up_in": i["peer_up"][0].reshape(NK, P, D)}
    arrays = {k: np.ascontiguousarray(v) for k, v in arrays.items()}
    nc = bacc.Bacc("TRN2", target_bir_lowering=False, num_devices=1)
    args = [nc.dram_tensor(k, v.shape, mybir.dt.from_np(v.dtype), kind="ExternalInput").ap() for k, v in arrays.items()]
    args.append(nc.dram_tensor("out", (SEQ, D), F32, kind="ExternalOutput").ap())
    args.append(nc.dram_tensor("gate_dram", (P, NK, SEQ), F32, kind="Internal").ap())
    args.append(nc.dram_tensor("hid_dram", (EARLY, P, SEQ), F32, kind="Internal").ap())
    build(nc, *args)
    r = run_bass_kernel_spmd(nc, [arrays], core_ids=[0])
    return r.results[0]["out"].reshape(1, SEQ, D)
```

```python
from contextlib import ExitStack

import concourse.bass as bass
from concourse import mybir

F32 = mybir.dt.float32
F32R = mybir.dt.float32r
U32 = mybir.dt.uint32
ALU = mybir.AluOpType
ACT = mybir.ActivationFunctionType
AX_X = mybir.AxisListType.X

P = 128
D = 1024
KC = D // P
SEQ = 512
NT = SEQ // P
NM = 256
MT = NM // P
CW = 512
CC = CW // P
HH = 4
CH = 64
NCH = SEQ // CH
MH = 4
DH = D // MH
PH = 8
NK = 128
TK = 16
NEG = -3.0e38
EPS = 1e-6

RING = 4
FRONT = 84
EXP_AT = (8, 16, 28, 36)
TURN_AT = (12, 20, 32, 40)
AHEAD = TURN_AT[-1]
DURING = AHEAD + 16
EARLY = DURING + 8
GT = 2
GROUPS = NK // GT
FIRST_D = EARLY // GT - 1
TB = 8
HOTS = 4

V_MIX, V_CONV, V_HGRN, V_LB0, V_LB1, V_ATT, V_MEM, V_FFN, V_CW = 0, 8, 12, 16, 20, 24, 32, 40, 48
NV = V_CW + 3 * CC


def build(nc, x_in, mem_in, vecs_in, final_in, front_w, keys_in, down_in, up_in, out, gate_dram, hid_dram):
    ctx = ExitStack()
    with ctx:
        def sem(name):
            return ctx.enter_context(nc.semaphore(name))

        KB = 256
        with ExitStack() as over:
            def halves(name, kb, shape, now):
                if kb > now:
                    over.enter_context(nc.sbuf_tensor(f"pad{kb}", [P, (kb - now) * KB], F32))
                return [over.enter_context(nc.sbuf_tensor(name + half, [P] + shape, F32R)) for half in ("_high", "_low")]

            w_half = halves("w", 44, [2, D], 0)
            hT_half = halves("hT", 60, [KC, SEQ], 60)
            up_half = halves("up", 140, [4, D], 92)
            wgt_half = halves("wgt", 172, [4, SEQ], 172)
            memT_half = halves("memT", 188, [KC, NM], 188)
        kept = ctx.enter_context(nc.sbuf_tensor("kept", [P, 44 * KB], F32))
        ctx.enter_context(nc.sbuf_tensor("under_w", [P, 16 * KB], F32))
        arena = ctx.enter_context(nc.sbuf_tensor("arena", [P, 146 * KB], F32))
        psum = ctx.enter_context(nc.psum_tensor("psum", [P, 8, 512], F32))

        def at(kb, n, *dims):
            where, kb = (kept, kb) if kb < 44 else (arena, kb - 60)
            a = where[:, int(kb * KB):int(kb * KB) + n]
            if len(dims) == 2:
                return a.rearrange("p (a b) -> p a b", a=dims[0])
            if len(dims) == 3:
                return a.rearrange("p (a b c) -> p a b c", a=dims[0], b=dims[1])
            return a

        x = at(0, NT * D, NT, D)
        vec = at(16, NV)
        ident = at(16.5, P)
        ones = at(17, P)
        iota = at(17.5, P)
        causal = at(18, P)
        fin_w = at(18.5, D)
        ss = at(22.5, 16)
        ms = at(22.5625, 16)
        rt = at(22.625, 16)
        rs = at(22.6875, 16)
        lbm = at(22.75, 32)
        lb, oml = lbm[:, 20:24], lbm[:, 24:28]
        decay = at(23, HH * NCH, HH, NCH)
        gend = at(27.5, HH * NCH)
        mx, nmx, den, rden = (at(23.25 + 0.0625 * j, 16) for j in range(4))
        junk = at(23.5, D)
        ring = at(28, RING * D, RING, D)
        hn = at(92, NT * D, NT, D)
        proj = at(108, 24 * SEQ, 24, SEQ)
        pQ, pF, pG, pB, pC, pV = (proj[:, 4 * j:4 * j + 4, :] for j in range(6))
        iN = at(156, NT * CW, NT, CW)
        mem = at(164, MT * D, MT, D)
        KT = at(172, KC * NM, KC, NM)
        Vm = at(180, MT * D, MT, D)
        kk = at(92, HH * SEQ, HH, SEQ)
        G = at(100, HH * SEQ, HH, SEQ)
        expN = at(164, HH * SEQ, HH, SEQ)
        csq = at(76, CC * SEQ, CC, SEQ)
        aT = at(84, HH * SEQ, HH, SEQ)
        keN = at(60, HH * SEQ, HH, SEQ)
        S = at(92, HH * NCH * P, HH, NCH, P)
        sq, rinv = expN, pF
        reset = at(204, SEQ)
        qT = at(108, KC * SEQ, KC, SEQ)
        prob = at(124, 2 * NT * NM, 2, NT, NM)
        pT = at(132, 2 * MT * SEQ, 2, MT, SEQ)
        qpT = at(108, 16 * SEQ, 16, SEQ)
        score = at(140, NT * 16 * NK, NT, 16 * NK)
        keysT = at(172, 16 * NK, 16, NK)
        cand = at(108, PH * TK * TK, PH, TK * TK)
        onehot = at(116, PH * TK * TK, PH, TK * TK)
        top = at(124, 16 * TK, 16, TK)
        topi = at(125, 16 * TK, 16, TK)
        topf = at(126, 16 * TK, 16, TK)
        best = at(127, PH * TK, PH, TK)
        pos = at(127.5, PH * TK, PH, TK)
        posd = at(128, PH * TK, PH, TK)
        posf = at(128.5, 2 * PH * TK, 2, PH, TK)
        ebest = at(129.5, PH * TK, PH, TK)
        hk = at(130, 3 * P, 3, P)
        esum = at(131.5, 16)
        hkT = at(132, 3 * SEQ, 3, SEQ)
        hid = [at(138, SEQ), at(204, SEQ)]
        hot = at(92, HOTS * 2 * TB * P, HOTS, 2, TB * P)
        stage = at(140, 2 * P * CH, 2, P, CH)
        uraw = at(92, 4 * D, 4, D)
        wraw = at(108, 2 * SEQ, 2, SEQ)
        gates = at(188, 4 * SEQ, 2, NCH, GT * CH)
        hidr = at(196, 4 * SEQ, 4, SEQ)

        ld_mem, ld_vec, ld_fin, ld_keys = (sem(n) for n in ("ld_mem", "ld_vec", "ld_fin", "ld_keys"))
        ld_x = [sem(f"ld_x{t}") for t in range(NT)]
        wt = [sem(f"weight_slot{s}") for s in range(RING)]
        block_used = sem("block_used")
        high_ready = sem("high_ready")
        low_ready = sem("low_ready")
        up_high, up_low = sem("up_high"), sem("up_low")
        consts = sem("consts")
        class Norm:
            def __init__(self, name, src, dst, hT, tiles, gain):
                self.src, self.dst, self.hT, self.tiles, self.gain = src, dst, hT, tiles, gain
                self.sumsq, self.mean, self.root, self.h, self.tr, self.high, self.ready = (
                    sem(f"{name}_{s}") for s in ("sumsq", "mean", "root", "h", "transposed", "high", "ready"))

        mixn = Norm("mix", x, hn, hT_half, NT, V_MIX)
        memn = Norm("mem", mem, mem, memT_half, MT, V_MEM)
        attn = Norm("att", x, hn, hT_half, NT, V_ATT)
        ffnn = Norm("ffn", x, hn, hT_half, NT, V_FFN)
        bank_free = sem("bank_free")
        i_out, k_out, v_out = sem("i_out"), sem("k_out"), sem("v_out")
        i_done, v_done = sem("i_done"), sem("v_done")
        lb_diff, lb_exp, silu_done = sem("lb_diff"), sem("lb_exp"), sem("silu_done")
        exp_fqg, fg_ready, logf_ready, G_ready, expG_ready, qk_ready = (
            sem(n) for n in ("exp_fqg", "fg_ready", "logf_ready", "G_ready", "expG_ready", "qk_ready"))
        conv_y, conv_sq, conv_sum, conv_root = (sem(n) for n in ("conv_y", "conv_sq", "conv_sum", "conv_root"))
        a_zero = sem("a_zero")
        ke_tr, ke_out, a_done, a_ready = (sem(n) for n in ("ke_tr", "ke_out", "a_done", "a_ready"))
        u_done, s_ready, o_done, o_sq, o_sum, o_root = (
            sem(n) for n in ("u_done", "s_ready", "o_done", "o_sq", "o_sum", "o_root"))
        mix_done, x_mixed = sem("mix_done"), sem("x_mixed")
        q_out, sc_done, sc_max, sc_exp, p_ready, p_tr, pT_out, ao_done, ao_out = (
            sem(n) for n in ("q_out", "sc_done", "sc_max", "sc_exp", "p_ready", "p_tr", "pT_out", "ao_done", "ao_out"))
        att_done, x_att = sem("att_done"), sem("x_att")
        qp_out, pk_done, pk_out = sem("qp_out"), sem("pk_done"), sem("pk_out")
        best_ready, e_ready, hk_ready, hk_tr, hkT_out = (
            sem(n) for n in ("best_ready", "e_ready", "hk_ready", "hk_tr", "hkT_out"))
        hot_eq, hot_ready, gate_done, gate_out = (sem(n) for n in ("hot_eq", "hot_ready", "gate_done", "gate_out"))
        stored = [sem(f"gates_stored{s}") for s in range(2)]
        ld_up = [sem(f"ld_up{s}") for s in range(4)]
        ld_gate = [sem(f"ld_gate{s}") for s in range(4)]
        ld_hid = [sem(f"ld_hid{s}") for s in range(4)]
        hid_stored = [sem(f"hid_stored{s}") for s in range(2)]
        gelu_out, w_raw, w_high, w_ready, up_done, x_added = (
            sem(n) for n in ("gelu_out", "w_raw", "w_high", "w_ready", "up_done", "x_added"))
        ao_high, y_ready = sem("ao_high"), sem("y_ready")
        fin_sq, fin_mean, fin_root, fin_y, out_stored = (
            sem(n) for n in ("fin_sq", "fin_mean", "fin_root", "fin_y", "out_stored"))
        dve_step, act_step, pool_step = sem("dve_step"), sem("act_step"), sem("pool_step")

        class Steps:
            def __init__(self, eng, own):
                self.eng, self.own, self.n = eng, own, 0

            def put(self, ins):
                ins.then_inc(self.own, 1)
                self.n += 1

            def end(self):
                self.eng.wait_ge(self.own, self.n)

            def __call__(self, ins):
                self.put(ins)
                self.end()

        block = ctx.enter_context(nc.Block())

        @block.sync
        def _(sp):
            def load_block(b, s):
                sp.dma_start(ring[:, s, :], front_w[bass.ds(b, 1)].rearrange("b p n -> (b p) n")).then_inc(wt[s], 16)

            def load_down(i, s):
                sp.dma_start(ring[:, s, :], down_in[bass.ds(i, 1)].rearrange("b p n -> (b p) n")).then_inc(wt[s], 16)

            for s in range(RING):
                sp.wait_ge(ld_x[1 + 2 * (s // 2)], 16)
                load_block(s, s)
            sp.dma_start(mem, mem_in.rearrange("(t p) d -> p t d", p=P)).then_inc(ld_mem, 16)
            sp.dma_start(fin_w, final_in.to_broadcast([P, D])).then_inc(ld_fin, 16)
            with sp.Fori(1, FRONT // RING) as r:
                for s in range(RING):
                    sp.wait_ge(low_ready, r * RING + (s + 1 - RING))
                    load_block(r * RING + s, s)
            with sp.Fori(0, EARLY // RING) as r:
                for s in range(RING):
                    sp.wait_ge(low_ready, r * RING + (FRONT + s + 1 - RING))
                    load_down(r * RING + s, s)

            def load_up(i, s):
                sp.dma_start(uraw[:, s, :], up_in[bass.ds(i, 1)].rearrange("b p n -> (b p) n")).then_inc(ld_up[s], 16)

            def load_gates(i, s):
                sp.dma_start(gates[:, s], gate_dram[:, :, bass.ds(i * CH, GT * CH)]).then_inc(ld_gate[s], 16)

            def load_hid(i, s):
                sp.dma_start(hidr[:, s, :], hid_dram[bass.ds(i, 1)].rearrange("b p n -> (b p) n")).then_inc(ld_hid[s], 16)

            sp.wait_ge(gate_done, SEQ // TB)
            for s in range(4):
                load_up(s, s)
            for s in range(2):
                sp.wait_ge(stored[s], 16 * NT)
                sp.wait_ge(hid_stored[s], 16 * DURING // 2)
            for s in range(4):
                if s % 2 == 0:
                    load_gates(s, s // 2)
                load_hid(s, s)
            for s in range(RING):
                sp.wait_ge(low_ready, EARLY + FRONT + s + 1 - RING)
                load_down(EARLY + s, s)
            for s in range(2):
                sp.wait_ge(hid_stored[s], 16 * EARLY // 2)
            with sp.Fori(1, EARLY // 4) as r:
                for s in range(4):
                    sp.wait_ge(up_low, r * 4 + (s - 3))
                    load_up(r * 4 + s, s)
                    sp.wait_ge(w_ready, r * 4 + (s - 3))
                    load_hid(r * 4 + s, s)
                    if s % 2:
                        load_gates(r * 4 + (s - 1), s // 2)
            with sp.Fori(EARLY // 4, NK // 4 - 1) as r:
                for s in range(4):
                    sp.wait_ge(up_low, r * 4 + (s - 3))
                    load_up(r * 4 + s, s)
                    if s % 2:
                        sp.wait_ge(w_ready, r * 4 + (s - 3))
                        load_gates(r * 4 + (s - 1), s // 2)
                    sp.wait_ge(low_ready, r * 4 + (FRONT + s + 1))
                    load_down(r * 4 + (s + 4), s)
            for s in range(4):
                sp.wait_ge(up_low, NK - 4 + (s - 3))
                load_up(NK - 4 + s, s)
                if s % 2:
                    sp.wait_ge(w_ready, NK - 4 + (s - 3))
                    load_gates(NK - 5 + s, s // 2)
            for t in range(NT):
                sp.wait_ge(fin_y, t + 1)
                sp.dma_start(out[t * P:(t + 1) * P, :], hn[:, t, :]).then_inc(out_stored, 16)
            sp.wait_ge(out_stored, 16 * NT)

        @block.gpsimd
        def _(pool):
            step = Steps(pool, pool_step)
            nc.gpsimd.memset(ones, 1.0).then_inc(consts, 1)
            step(nc.gpsimd.memset(ident, 0.0))
            nc.gpsimd.affine_select(out=ident, in_=ident, compare_op=ALU.not_equal, fill=1.0, base=0,
                                    pattern=[[-1, P]], channel_multiplier=1).then_inc(consts, 1)
            step(nc.gpsimd.memset(causal, 1.0))
            step(nc.gpsimd.affine_select(out=causal, in_=causal, compare_op=ALU.is_ge, fill=0.0, base=0,
                                         pattern=[[1, P]], channel_multiplier=-1))
            nc.gpsimd.affine_select(out=causal[:, CH:P], in_=causal[:, CH:P], compare_op=ALU.is_ge, fill=0.0,
                                    base=-CH, pattern=[[0, P - CH]], channel_multiplier=1).then_inc(consts, 1)
            nc.gpsimd.iota(iota, pattern=[[1, P]], base=0, channel_multiplier=0,
                           allow_small_or_imprecise_dtypes=True).then_inc(consts, 1)
            step(nc.gpsimd.memset(reset, 1.0))
            nc.gpsimd.memset(reset.rearrange("p (c t) -> p c t", t=CH)[:, :, 0:1], 0.0).then_inc(consts, 1)

            def low(b, s):
                pool.wait_ge(high_ready, b + 1)
                nc.gpsimd.tensor_tensor(w_half[1][:, s % 2, :], ring[:, s, :], w_half[0][:, s % 2, :].bitcast(F32),
                                        ALU.subtract).then_inc(low_ready, 1)

            def low_up(i, s):
                pool.wait_ge(up_high, i + 1)
                nc.gpsimd.tensor_tensor(up_half[1][:, s, :], uraw[:, s, :], up_half[0][:, s, :].bitcast(F32),
                                        ALU.subtract).then_inc(up_low, 1)

            with pool.Fori(0, 7) as r:
                for s in range(4):
                    low(r * 4 + s, s)
            low(28, 0)
            low(29, 1)
            pool.wait_ge(block_used, 28)
            nc.gpsimd.memset(aT, 0.0).then_inc(a_zero, 1)
            low(30, 2)
            low(31, 3)
            with pool.Fori(8, (FRONT + AHEAD) // 4) as r:
                for s in range(4):
                    low(r * 4 + s, s)
            for s in range(2):
                low(FRONT + AHEAD + s, s)
            for g in range(SEQ // TB // HOTS):
                for n in range(g * HOTS, (g + 1) * HOTS):
                    rows = hot[:, n % HOTS, 1, :].rearrange("p (n j) -> p n j", n=TB)
                    gate = hkT[:, 2, n * TB:(n + 1) * TB].rearrange("p (n j) -> p n j", j=1).to_broadcast([P, TB, P])
                    pool.wait_ge(hot_eq, n + 1)
                    nc.gpsimd.tensor_tensor(rows, rows, gate, ALU.mult).then_inc(hot_ready, 1)
                    if g and n % HOTS == 1:
                        low(FRONT + AHEAD + 1 + g, (1 + g) % 4)
            for k in range(EARLY - 4 - DURING + 1):
                low(FRONT + DURING + 1 + k, (1 + k) % 4)
            for i in range(4):
                if i != 1:
                    for k in ((0, 1), (), (2,), (3,))[i]:
                        low(FRONT + EARLY - 2 + k, (2 + k) % 4)
                low_up(i, i)
            with pool.Fori(1, EARLY // 4) as r:
                for s in range(4):
                    low_up(r * 4 + s, s)

            def both(i0, slot):
                for k in range(2):
                    low(i0 + (FRONT + 2 + k), (FRONT + slot + 2 + k) % 4)
                for k in range(2):
                    low_up(i0 + k, (slot + k) % 4)

            both(EARLY, 0)
            with pool.Fori(0, (NK - EARLY) // 4 - 1) as r:
                both(r * 4 + (EARLY + 2), 2)
                both(r * 4 + (EARLY + 4), 0)
            for k in range(2):
                low_up(NK - 2 + k, 2 + k)

        @block.scalar
        def _(act):
            for t in range(NT):
                act.dma_start(x[:, t, :], x_in[t * P:(t + 1) * P, :]).then_inc(ld_x[t], 16)
            act.dma_start(vec, vecs_in).then_inc(ld_vec, 16)
            act.sem_inc(bank_free, 4)
            act.sem_inc(gelu_out, 2)
            act.sem_inc(gate_out, 2)

            def table(function):
                nc.scalar.activation(rt[:, 15:16], ones[:, 0:1], function).then_inc(act_step, 1)

            def norm(u, col, landed):
                for t in range(u.tiles):
                    act.wait_ge(landed[t], 16)
                    nc.scalar.activation(junk, u.src[:, t, :], ACT.Square, accum_out=ss[:, col + t:col + t + 1])\
                        .then_inc(u.sumsq, 1)
                    act.wait_ge(u.sumsq, t + 1)
                root(u, col)

            def root(u, col):
                act.wait_ge(u.mean, 1)
                nc.scalar.activation(rt[:, col:col + u.tiles], ms[:, col:col + u.tiles], ACT.Sqrt).then_inc(u.root, 1)

            def square(u, added, hf, tiles):
                for t in tiles:
                    act.wait_ge(added, hf * NT + t + 1)
                    nc.scalar.activation(junk[:, 0:512], x[:, t, hf * 512:(hf + 1) * 512], ACT.Square,
                                         accum_out=ss[:, 8 * hf + t:8 * hf + t + 1]).then_inc(u.sumsq, 1)
                    act.wait_ge(u.sumsq, hf * NT + t + 1)

            def norm_high(u):
                for k in range(KC):
                    act.wait_ge(u.tr, k + 1)
                    nc.scalar.activation(u.hT[0][:, k, :], psum[:, 4 + k % 4, 0:u.tiles * P], ACT.Copy,
                                         scale=vec[:, u.gain + k:u.gain + k + 1]).then_inc(u.high, 1)

            def high(b, s, landed):
                act.wait_ge(wt[s], landed)
                nc.scalar.activation(w_half[0][:, s % 2, :], ring[:, s, :], ACT.Copy).then_inc(high_ready, 1)

            def high_up(i, s, landed):
                act.wait_ge(ld_up[s], landed)
                nc.scalar.activation(up_half[0][:, s, :], uraw[:, s, :], ACT.Copy).then_inc(up_high, 1)

            def ahead(b):
                act.wait_ge(block_used, b + 1)
                high(b + 2, (b + 2) % 4, 16 * ((b + 2) // 4 + 1))

            act.wait_ge(consts, 1)
            table(ACT.Sqrt)
            norm(mixn, 0, ld_x)
            high(0, 0, 16)
            high(1, 1, 16)
            act.wait_ge(ld_vec, 16)
            norm_high(mixn)
            act.wait_ge(lb_diff, 1)
            nc.scalar.activation(lbm[:, 4:12], lbm[:, 4:12], ACT.Exp).then_inc(lb_exp, 1)
            norm(memn, 4, [ld_mem] * MT)
            with act.Fori(0, 3) as r:
                for s in range(4):
                    act.wait_ge(block_used, r * 4 + (s + 1))
                    high(None, (s + 2) % 4, r * 16 + 16 * ((s + 2) // 4 + 1))
                    nc.scalar.activation(proj[:, bass.ds(r * 4 + s, 1), :], psum[:, s:s + 1, :], ACT.Copy)\
                        .then_inc(bank_free, 1)
            act.wait_ge(bank_free, 16)
            for n, (a, b) in enumerate(((pF, pF), (G, pQ), (pV, pG))):
                ahead(12 + n)
                nc.scalar.activation(a, b, ACT.Exp, scale=-1.0).then_inc(exp_fqg, 1)
            ahead(15)
            act.wait_ge(i_done, 1)
            for t in range(NT):
                nc.scalar.activation(iN[:, t, :], psum[:, 4 + t, :], ACT.Copy).then_inc(i_out, 1)
            for b in range(12):
                ahead(16 + b)
                if b == 8:
                    act.wait_ge(silu_done, 1)
                nc.scalar.activation(proj[:, 12 + b, :], psum[:, b % 4, :], ACT.Copy).then_inc(bank_free, 1)
                if b == 1:
                    norm_high(memn)
                if b == 3:
                    act.wait_ge(fg_ready, 1)
                    nc.scalar.activation(pF, pF, ACT.Ln).then_inc(logf_ready, 1)
                if b == 6:
                    act.wait_ge(G_ready, 1)
                    nc.scalar.activation(pF, G, ACT.Exp).then_inc(expG_ready, 1)
                if b == 7:
                    act.wait_ge(memn.tr, KC)
                    nc.scalar.activation(expN, G, ACT.Exp, scale=-1.0).then_inc(expG_ready, 1)
                if b == 9:
                    act.wait_ge(G_ready, 2)
                    nc.scalar.activation(G, G, ACT.Exp).then_inc(expG_ready, 1)
            def keys_out(block, b, bank):
                ahead(block)
                nc.scalar.activation(KT[:, b, :], psum[:, bank, 0:NM], ACT.Copy).then_inc(k_out, 1)

            def values_out(hf, bank):
                act.wait_ge(v_done, hf + 1)
                for t in range(MT):
                    nc.scalar.activation(Vm[:, t, hf * 512:(hf + 1) * 512], psum[:, bank + t, :], ACT.Copy)\
                        .then_inc(v_out, 1)

            for h in range(HH):
                act.wait_ge(ke_tr, h + 1)
                nc.scalar.activation(keN[:, h, :], psum[:, h, :], ACT.Copy).then_inc(ke_out, 1)
            for b in range(4):
                act.wait_ge(conv_y, b + 1)
                nc.scalar.activation(csq[:, b, :], pF[:, b, :], ACT.Square).then_inc(conv_sq, 1)
                keys_out(28 + b, b, b)
            act.wait_ge(conv_sum, 1)
            nc.scalar.activation(junk[:, 0:SEQ], psum[:, 4, :], ACT.Copy, scale=1.0 / CW, bias=EPS).then_inc(act_step, 1)
            act.wait_ge(act_step, 2)
            nc.scalar.activation(junk[:, SEQ:2 * SEQ], junk[:, 0:SEQ], ACT.Sqrt).then_inc(conv_root, 1)
            for b in range(4):
                ahead(32 + b)
            values_out(0, 6)
            for b in (4, 5):
                keys_out(32 + b, b, b)
            for h in range(HH):
                act.wait_ge(o_done, h + 1)
                nc.scalar.activation(sq[:, h, :], psum[:, 4 + h, :], ACT.Square).then_inc(o_sq, 1)
            for h in range(HH):
                act.wait_ge(o_sum, h + 1)
                nc.scalar.activation(rinv[:, h, :], psum[:, 2 + h % 2, :], ACT.Copy, scale=1.0 / P, bias=EPS)\
                    .then_inc(act_step, 1)
                act.wait_ge(act_step, 3 + h)
                nc.scalar.activation(rinv[:, h, :], rinv[:, h, :], ACT.Sqrt).then_inc(o_root, 1)
                if h % 2:
                    keys_out(38 + h // 2, 6 + h // 2, h // 2)
            for b in range(40, 45):
                ahead(b)
            square(attn, x_mixed, 0, (0, 1))
            ahead(45)
            square(attn, x_mixed, 0, (2, 3))
            ahead(46)
            square(attn, x_mixed, 1, (0, 1, 2))
            ahead(47)
            ahead(48)
            square(attn, x_mixed, 1, (3,))
            root(attn, 0)
            for b in (49, 50, 51):
                ahead(b)
            norm_high(attn)
            values_out(1, 2)
            act.wait_ge(act_step, 6)
            table(ACT.Exp)
            for b in range(KC):
                act.wait_ge(block_used, 52 + b + 1)
                nc.scalar.activation(qT[:, b, :], psum[:, b % 4, :], ACT.Copy).then_inc(q_out, 1)
                ahead(52 + b)
            def attention_exp(h):
                act.wait_ge(sc_max, h + 1)
                for t in range(NT):
                    bank = 2 * (h % 2) + t // 2
                    nc.scalar.activation(prob[:, h % 2, t, :], psum[:, bank, (t % 2) * NM:(t % 2 + 1) * NM], ACT.Exp,
                                         scale=DH ** -0.5, bias=nmx[:, 4 * (h % 2) + t:4 * (h % 2) + t + 1],
                                         accum_out=den[:, 4 * (h % 2) + t:4 * (h % 2) + t + 1]).then_inc(sc_exp, 1)

            attention_exp(0)
            for h in range(MH):
                for m in range(MT):
                    act.wait_ge(p_tr, MT * h + m + 1)
                    nc.scalar.activation(pT[:, h % 2, m, :], psum[:, 4 + m, :], ACT.Copy).then_inc(pT_out, 1)
                if h + 1 < MH:
                    attention_exp(h + 1)
                for c in range(2):
                    act.wait_ge(ao_done, 2 * h + c + 1)
                    nc.scalar.activation(hT_half[0][:, 2 * h + c, :], psum[:, 6 + c, :], ACT.Copy).then_inc(ao_high, 1)
            act.dma_start(keysT, keys_in).then_inc(ld_keys, 16)
            act.wait_ge(act_step, 7)
            table(ACT.Sqrt)
            for b in range(60, 67):
                ahead(b)
                if b in (64, 65):
                    square(ffnn, x_att, 0, (2 * (b - 64), 2 * (b - 64) + 1))
            square(ffnn, x_att, 1, range(NT))
            root(ffnn, 0)
            ahead(67)
            norm_high(ffnn)
            with act.Fori(0, 4) as r:
                for s in range(4):
                    act.wait_ge(block_used, r * 4 + (68 + s + 1))
                    nc.scalar.activation(qpT[:, bass.ds(r * 4 + s, 1), :], psum[:, s:s + 1, :], ACT.Copy)\
                        .then_inc(qp_out, 1)
                    high(None, (s + 2) % 4, r * 16 + 16 * ((68 + s + 2) // 4 + 1))
            for b in range(16):
                act.wait_ge(pk_done, b + 1)
                nc.scalar.activation(score[:, b // 4, (b % 4) * 512:(b % 4 + 1) * 512], psum[:, 4 + b % 4, :], ACT.Copy)\
                    .then_inc(pk_out, 1)
            def early(i, s, landed, used, slot_free, done):
                act.wait_ge(block_used, used)
                high(None, (s + 2) % 4, landed)
                if slot_free is not None:
                    act.wait_ge(hid_stored[s % 2], slot_free)
                nc.scalar.activation(hid[s % 2], psum[:, 4 + s % 2, :], ACT.Gelu).then_inc(gelu_out, 1)
                act.wait_ge(gelu_out, done)
                act.dma_start(hid_dram[bass.ds(i, 1)].rearrange("b p n -> (b p) n"), hid[s % 2])\
                    .then_inc(hid_stored[s % 2], 16)

            def early_at(i):
                early(i, i % 4, 16 * ((FRONT + i + 2) // 4 + 1), FRONT + i + 1, 16 * (i // 2) if i > 1 else None, i + 3)

            def early_tiles(i0, i1):
                with act.Fori(i0 // 4, i1 // 4) as r:
                    for s in range(4):
                        early(r * 4 + s, s, r * 16 + 16 * ((FRONT + s + 2) // 4 + 1), r * 4 + (FRONT + s + 1),
                              r * 32 + 16 * (s // 2), r * 4 + (s + 3))

            for t in range(NT):
                if t == 0:
                    for i in range(EXP_AT[0]):
                        early_at(i)
                else:
                    early_tiles(TURN_AT[t - 1], EXP_AT[t])
                act.wait_ge(best_ready, t + 1)
                nc.scalar.activation(ebest, ebest, ACT.Exp).then_inc(e_ready, 1)
                early_tiles(EXP_AT[t], TURN_AT[t])
                act.wait_ge(hk_tr, t + 1)
                nc.scalar.activation(hkT[:, :, t * P:(t + 1) * P],
                                     psum[:, 6, 0:3 * P].rearrange("p (a b) -> p a b", a=3), ACT.Copy)\
                    .then_inc(hkT_out, 1)
            for c in range(NCH):
                if c >= 2:
                    act.wait_ge(stored[c % 2], 16 * (c // 2))
                for k in range(CH // TB):
                    n = c * (CH // TB) + k
                    if n % HOTS == 0:
                        early_at(AHEAD + n // HOTS)
                    act.wait_ge(gate_done, n + 1)
                    nc.scalar.activation(
                        stage[:, c % 2, :, k * TB:(k + 1) * TB].rearrange("p i n -> p n i"),
                        psum[:, 2 * (n % 2):2 * (n % 2) + 2, :].rearrange("p b (n i) -> p (b n) i", i=P), ACT.Copy)\
                        .then_inc(gate_out, 1)
                act.wait_ge(gate_out, (c + 1) * (CH // TB) + 2)
                act.dma_start(gate_dram[:, c, :], stage[:, c % 2].rearrange("p i n -> p (i n)"))\
                    .then_inc(stored[c % 2], 16)
            for i in range(DURING, EARLY - 4):
                early_at(i)
            for i in range(4):
                early_at(EARLY - 4 + i)
                if i == 1:
                    for s in range(2):
                        act.wait_ge(stored[s], 16 * NT)
                    high_up(0, 0, 16)
                if i:
                    high_up(i, i, 16)
            with act.Fori(1, EARLY // 4) as r:
                for s in range(4):
                    if s % 2 == 0:
                        act.wait_ge(up_done, r * 16 + (8 * (s // 2) - 8))
                    high_up(None, s, r * 16 + 16)

            def both(i0, slot, landed, used, up_free, last=False):
                for k in range(2):
                    act.wait_ge(block_used, used + k)
                    if not last:
                        high(None, (slot + 2 + k) % 4, landed)
                    act.wait_ge(w_ready, i0 + (k - 1))
                    nc.scalar.activation(hid[k], psum[:, 4 + k, :], ACT.Gelu).then_inc(gelu_out, 1)
                act.wait_ge(up_done, up_free)
                for k in range(2):
                    high_up(None, slot + k, landed - 16 * ((slot + 2) // 4) - 16 * (FRONT // 4))

            for s in range(2):
                act.wait_ge(hid_stored[s], 16 * EARLY // 2)
            both(EARLY, 0, 16 * ((FRONT + EARLY + 2) // 4 + 1), FRONT + EARLY + 1, 4 * EARLY - 8)
            with act.Fori(EARLY // 4, NK // 4 - 1) as r:
                both(r * 4 + 2, 2, r * 16 + (16 * (FRONT // 4) + 32), r * 4 + (FRONT + 3), r * 16)
                both(r * 4 + 4, 0, r * 16 + (16 * (FRONT // 4) + 32), r * 4 + (FRONT + 5), r * 16 + 8)
            both(NK - 2, 2, 16 * (NK // 4 + FRONT // 4) + 16, FRONT + NK - 1, 4 * NK - 16, last=True)
            act.wait_ge(act_step, 8)
            table(ACT.Sqrt)
            for t in range(NT):
                act.wait_ge(x_added, 8 * (GROUPS - 1) + 2 * t + 2 + 4)
                nc.scalar.activation(junk, x[:, t, :], ACT.Square, accum_out=ss[:, t:t + 1]).then_inc(fin_sq, 1)
                act.wait_ge(fin_mean, t + 1)
                nc.scalar.activation(rt[:, t:t + 1], ms[:, t:t + 1], ACT.Sqrt).then_inc(fin_root, 1)

        @block.vector
        def _(dve):
            step = Steps(dve, dve_step)
            dve.sem_inc(x_added, 4)

            def norm_rows(u, col, halved=False):
                sums = ss[:, col:col + u.tiles]
                if halved:
                    dve.wait_ge(u.sumsq, 2 * NT)
                    sums = ms[:, col:col + NT]
                    step(nc.vector.tensor_tensor(sums, ss[:, col:col + NT], ss[:, 8 + col:8 + col + NT], ALU.add))
                else:
                    dve.wait_ge(u.sumsq, u.tiles)
                nc.vector.tensor_scalar(ms[:, col:col + u.tiles], sums, 1.0 / D, EPS,
                                        ALU.mult, ALU.add).then_inc(u.mean, 1)
                dve.wait_ge(u.root, 1)
                step(nc.vector.reciprocal(rs[:, col:col + u.tiles], rt[:, col:col + u.tiles]))
                for c in (slice(0, D // 2), slice(D // 2, D)):
                    for t in range(u.tiles):
                        nc.vector.tensor_scalar(u.dst[:, t, c], u.src[:, t, c], rs[:, col + t:col + t + 1], None, ALU.mult)\
                            .then_inc(u.h, 1)

            def norm_gain(u):
                for k in range(KC):
                    dve.wait_ge(u.high, k + 1)
                    nc.vector.scalar_tensor_tensor(u.hT[1][:, k, :], psum[:, 4 + k % 4, 0:u.tiles * P],
                                                   vec[:, u.gain + k:u.gain + k + 1], u.hT[0][:, k, :].bitcast(F32),
                                                   ALU.mult, ALU.subtract).then_inc(u.ready, 1)

            dve.wait_ge(ld_vec, 16)
            norm_rows(mixn, 0)
            norm_gain(mixn)
            l0, l1 = vec[:, V_LB0:V_LB0 + HH], vec[:, V_LB1:V_LB1 + HH]
            step(nc.vector.tensor_tensor(lbm[:, 0:4], l0, l1, ALU.max))
            step(nc.vector.tensor_tensor(lbm[:, 4:8], l0, lbm[:, 0:4], ALU.subtract))
            nc.vector.tensor_tensor(lbm[:, 8:12], l1, lbm[:, 0:4], ALU.subtract).then_inc(lb_diff, 1)
            dve.wait_ge(lb_exp, 1)
            step(nc.vector.tensor_tensor(lbm[:, 12:16], lbm[:, 4:8], lbm[:, 8:12], ALU.add))
            step(nc.vector.reciprocal(lbm[:, 16:20], lbm[:, 12:16]))
            step(nc.vector.tensor_tensor(lb, lbm[:, 4:8], lbm[:, 16:20], ALU.mult))
            step(nc.vector.tensor_scalar(oml, lb, -1.0, 1.0, ALU.mult, ALU.add))
            norm_rows(memn, 4)
            dve.wait_ge(exp_fqg, 1)
            step(nc.vector.tensor_scalar(pF, pF, 1.0, None, ALU.add))
            step(nc.vector.reciprocal(pF, pF))
            for h in range(HH):
                step.put(nc.vector.tensor_scalar(pF[:, h, :], pF[:, h, :], oml[:, h:h + 1], lb[:, h:h + 1],
                                                 ALU.mult, ALU.add))
            step.end()
            nc.vector.tensor_scalar(kk, pF, -1.0, 1.0, ALU.mult, ALU.add).then_inc(fg_ready, 1)
            norm_gain(memn)

            def silu(e, a, n):
                dve.wait_ge(exp_fqg, n)
                step(nc.vector.tensor_scalar(e, e, 1.0, None, ALU.add))
                step(nc.vector.reciprocal(e, e))
                step(nc.vector.tensor_tensor(a, a, e, ALU.mult))

            silu(G, pQ, 2)
            dve.wait_ge(consts, 5)
            dve.wait_ge(logf_ready, 1)
            for h in range(HH):
                step.put(nc.vector.tensor_tensor_scan(G[:, h, :], reset, pF[:, h, :], 0.0, ALU.mult, ALU.add))
            step.end()
            Gc = G.rearrange("p h (c t) -> p (h c) t", t=CH)
            nc.vector.tensor_copy(gend.rearrange("p (c t) -> p c t", t=1), Gc[:, :, CH - 1:CH]).then_inc(G_ready, 1)
            dve.wait_ge(exp_fqg, 3)
            step(nc.vector.tensor_scalar(pV, pV, 1.0, None, ALU.add))
            step(nc.vector.reciprocal(pV, pV))
            nc.vector.tensor_tensor(pG, pG, pV, ALU.mult).then_inc(silu_done, 1)
            dve.wait_ge(G_ready, 1)
            dve.wait_ge(expG_ready, 2)
            nc.vector.tensor_tensor(Gc, gend.rearrange("p (c t) -> p c t", t=1).to_broadcast([P, HH * NCH, CH]), Gc,
                                    ALU.subtract).then_inc(G_ready, 1)
            step(nc.vector.tensor_copy(decay, pF.rearrange("p h (c t) -> p h c t", t=CH)[:, :, :, CH - 1]))
            step(nc.vector.tensor_tensor(pQ, pQ, pF, ALU.mult))
            step(nc.vector.tensor_tensor(expN, kk, expN, ALU.mult))
            dve.wait_ge(expG_ready, 3)
            nc.vector.tensor_tensor(G, kk, G, ALU.mult).then_inc(qk_ready, 1)
            dve.wait_ge(bank_free, 4 + 24)
            for c in range(CC):
                cw = [vec[:, V_CW + CC * j + c:V_CW + CC * j + c + 1] for j in range(3)]
                y, u = pF[:, c, :], pC[:, c, :]
                step(nc.vector.tensor_tensor(u, u, pV[:, c, :], ALU.mult))
                step(nc.vector.tensor_scalar(y, u, cw[2], None, ALU.mult))
                step(nc.vector.scalar_tensor_tensor(y[:, 1:], u[:, :SEQ - 1], cw[1], y[:, 1:], ALU.mult, ALU.add))
                step(nc.vector.scalar_tensor_tensor(y[:, 2:], u[:, :SEQ - 2], cw[0], y[:, 2:], ALU.mult, ALU.add))
                nc.vector.tensor_tensor(y, y, pB[:, c, :], ALU.mult).then_inc(conv_y, 1)
            dve.wait_ge(a_zero, 1)
            for h in range(HH):
                dve.wait_ge(a_done, h + 1)
                nc.vector.copy_predicated(
                    aT[:, h, :].rearrange("p (t c) -> p t c", c=P),
                    causal.bitcast(U32).rearrange("p (a c) -> p a c", a=1).to_broadcast([P, NT, P]),
                    psum[:, 4 + h, :].rearrange("p (t c) -> p t c", c=P)).then_inc(a_ready, 1)
            dve.wait_ge(conv_root, 1)
            dve.wait_ge(conv_y, CC)
            step(nc.vector.reciprocal(junk[:, 0:SEQ], junk[:, SEQ:2 * SEQ]))
            for c in range(CC):
                step.put(nc.vector.scalar_tensor_tensor(pB[:, c, :], pF[:, c, :], vec[:, V_CONV + c:V_CONV + c + 1],
                                                        junk[:, 0:SEQ], ALU.mult, ALU.mult))
            step.end()
            for h in range(HH):
                dve.wait_ge(u_done, h + 1)
                for n in range(NCH - 1):
                    u = psum[:, 2 * (h % 2) + n % 2, (n // 2) * P:(n // 2 + 1) * P]
                    if n == 0:
                        ins = nc.vector.tensor_copy(S[:, h, 1, :], u)
                    else:
                        ins = nc.vector.scalar_tensor_tensor(S[:, h, n + 1, :], S[:, h, n, :], decay[:, h, n:n + 1], u,
                                                             ALU.mult, ALU.add)
                    ins.then_inc(s_ready, 1)
                    dve.wait_ge(s_ready, h * (NCH - 1) + n + 1)
            def y_halves(c, y):
                step(nc.vector.tensor_copy(hT_half[0][:, c, :], y))
                nc.vector.tensor_tensor(hT_half[1][:, c, :], y, hT_half[0][:, c, :].bitcast(F32), ALU.subtract)\
                    .then_inc(y_ready, 1)

            for c in range(CC):
                y_halves(c, pB[:, c, :])
            for h in range(HH):
                dve.wait_ge(o_root, h + 1)
                step(nc.vector.reciprocal(rinv[:, h, :], rinv[:, h, :]))
                step(nc.vector.scalar_tensor_tensor(rinv[:, h, :], rinv[:, h, :], vec[:, V_HGRN + h:V_HGRN + h + 1],
                                                    pG[:, h, :], ALU.mult, ALU.mult))
                step(nc.vector.tensor_tensor(rinv[:, h, :], rinv[:, h, :], psum[:, 4 + h, :], ALU.mult))
                y_halves(CC + h, rinv[:, h, :])

            def residual(done, added):
                for hf in range(2):
                    for t in range(NT):
                        dve.wait_ge(done, 2 + t if hf else 1)
                        nc.vector.tensor_tensor(x[:, t, hf * 512:(hf + 1) * 512], x[:, t, hf * 512:(hf + 1) * 512],
                                                psum[:, 4 * hf + t, :], ALU.add).then_inc(added, 1)

            residual(mix_done, x_mixed)
            dve.wait_ge(x_mixed, 8)
            norm_rows(attn, 0, halved=True)
            norm_gain(attn)
            def score_max(h):
                o = 4 * (h % 2)
                dve.wait_ge(sc_done, h + 1)
                step(nc.vector.tensor_reduce(mx[:, o:o + NT].rearrange("p (a b) -> p a b", a=2),
                                             psum[:, 2 * (h % 2):2 * (h % 2) + 2, :].rearrange("p a (b m) -> p a b m", b=2),
                                             AX_X, ALU.max))
                nc.vector.tensor_scalar(nmx[:, o:o + NT], mx[:, o:o + NT], -DH ** -0.5, None, ALU.mult).then_inc(sc_max, 1)

            def probabilities(h):
                o = 4 * (h % 2)
                dve.wait_ge(sc_exp, NT * (h + 1))
                step(nc.vector.reciprocal(rden[:, o:o + NT], den[:, o:o + NT]))
                for t in range(NT):
                    nc.vector.tensor_scalar(prob[:, h % 2, t, :], prob[:, h % 2, t, :], rden[:, o + t:o + t + 1], None,
                                            ALU.mult).then_inc(p_ready, 1)

            def attended(h):
                for c in range(2):
                    dve.wait_ge(ao_high, 2 * h + c + 1)
                    nc.vector.tensor_tensor(hT_half[1][:, 2 * h + c, :], psum[:, 6 + c, :],
                                            hT_half[0][:, 2 * h + c, :].bitcast(F32), ALU.subtract).then_inc(ao_out, 1)

            score_max(0)
            for h in range(MH):
                probabilities(h)
                if h + 1 < MH:
                    score_max(h + 1)
                if h:
                    attended(h - 1)
            attended(MH - 1)
            residual(att_done, x_att)
            dve.wait_ge(x_att, 8)
            norm_rows(ffnn, 0, halved=True)
            norm_gain(ffnn)

            def top16(lists):
                for values, vals, index in lists:
                    step.put(nc.vector.max(vals[:, 0:8], values))
                step.end()
                for values, vals, index in lists:
                    step.put(nc.vector.max_index(index[:, 0:8], vals[:, 0:8], values))
                    step.put(nc.vector.match_replace(values, vals[:, 0:8], values, NEG))
                step.end()
                for values, vals, index in lists:
                    step.put(nc.vector.max(vals[:, 8:16], values))
                step.end()
                for values, vals, index in lists:
                    step.put(nc.vector.max_index(index[:, 8:16], vals[:, 8:16], values))
                step.end()

            dve.wait_ge(pk_out, 16)
            for t in range(NT):
                top16([(score[:, t, j * NK:(j + 1) * NK], top[:, j, :], topi[:, j, :].bitcast(U32)) for j in range(16)])
                step(nc.vector.tensor_copy(topf, topi.bitcast(U32)))
                half = top.rearrange("p (h q) k -> p h q k", q=2)
                step(nc.vector.tensor_tensor(
                    cand.rearrange("p h (a b) -> p h a b", a=TK),
                    half[:, :, 0, :].rearrange("p h (a b) -> p h a b", b=1).to_broadcast([P, PH, TK, TK]),
                    half[:, :, 1, :].rearrange("p h (a b) -> p h a b", a=1).to_broadcast([P, PH, TK, TK]), ALU.add))
                top16([(cand[:, h, :], best[:, h, :], pos[:, h, :].bitcast(U32)) for h in range(PH)])
                nc.vector.tensor_tensor(ebest, best, best[:, :, 0:1].to_broadcast([P, PH, TK]), ALU.subtract)\
                    .then_inc(best_ready, 1)
                step(nc.vector.tensor_scalar(posd.bitcast(U32), pos.bitcast(U32), 4, None, ALU.logical_shift_right))
                step(nc.vector.tensor_copy(posf[:, 0], posd.bitcast(U32)))
                step(nc.vector.tensor_scalar(posd.bitcast(U32), pos.bitcast(U32), TK - 1, None, ALU.bitwise_and))
                step(nc.vector.tensor_copy(posf[:, 1], posd.bitcast(U32)))
                halff = topf.rearrange("p (h q) k -> p h q k", q=2)
                if t:
                    dve.wait_ge(hk_tr, t)
                for q in range(2):
                    step(nc.vector.tensor_tensor(
                        onehot.rearrange("p h (k a) -> p (h k) a", a=TK),
                        posf[:, q].rearrange("p h (k b) -> p (h k) b", b=1).to_broadcast([P, PH * TK, TK]),
                        iota[:, 0:TK].rearrange("p (b a) -> p b a", b=1).to_broadcast([P, PH * TK, TK]), ALU.is_equal))
                    step(nc.vector.tensor_tensor(
                        onehot.rearrange("p h (k a) -> p h k a", a=TK),
                        onehot.rearrange("p h (k a) -> p h k a", a=TK),
                        halff[:, :, q, :].rearrange("p h (b a) -> p h b a", b=1).to_broadcast([P, PH, TK, TK]), ALU.mult))
                    step(nc.vector.tensor_reduce(hk[:, q, :], onehot.rearrange("p h (k a) -> p (h k) a", a=TK),
                                                 AX_X, ALU.add))
                dve.wait_ge(e_ready, t + 1)
                step(nc.vector.tensor_reduce(esum[:, 0:PH], ebest, AX_X, ALU.add))
                step(nc.vector.reciprocal(esum[:, 8:16], esum[:, 0:8]))
                nc.vector.tensor_tensor(hk[:, 2, :].rearrange("p (h k) -> p h k", k=TK), ebest,
                                        esum[:, 8:16].rearrange("p (h k) -> p h k", k=1).to_broadcast([P, PH, TK]),
                                        ALU.mult).then_inc(hk_ready, 1)

            def hots(n, s):
                for q in range(2):
                    ins = nc.vector.tensor_tensor(
                        hot[:, s, q, :].rearrange("p (n j) -> p n j", n=TB),
                        iota.rearrange("p (n j) -> p n j", n=1).to_broadcast([P, TB, P]),
                        hkT[:, q, bass.ds(n, TB)].rearrange("p (n j) -> p n j", j=1).to_broadcast([P, TB, P]),
                        ALU.is_equal)
                ins.then_inc(hot_eq, 1)

            dve.wait_ge(hkT_out, NT - 1)
            for s in range(HOTS):
                hots(s * TB, s)
            last = (SEQ - P) // TB // HOTS
            for r0, r1 in ((1, last), (last, SEQ // TB // HOTS)):
                if r0 == last:
                    dve.wait_ge(hkT_out, NT)
                with dve.Fori(r0, r1) as r:
                    for s in range(HOTS):
                        dve.wait_ge(gate_done, r * HOTS + (s + 1 - HOTS))
                        hots(r * (HOTS * TB) + s * TB, s)

            def weigh(i, s, landed, spilled):
                dve.wait_ge(ld_gate[s // 2], landed)
                if spilled:
                    dve.wait_ge(ld_hid[s], landed)
                else:
                    dve.wait_ge(gelu_out, i + 3)
                w = wraw[:, s % 2, :]
                nc.vector.tensor_tensor(
                    w.rearrange("p (c n) -> p c n", n=CH),
                    (hidr[:, s, :] if spilled else hid[s % 2]).rearrange("p (c n) -> p c n", n=CH),
                    gates[:, s // 2, :, (s % 2) * CH:(s % 2 + 1) * CH], ALU.mult).then_inc(w_raw, 1)
                dve.wait_ge(w_raw, i + 1)
                nc.vector.tensor_copy(wgt_half[0][:, s, :], w).then_inc(w_high, 1)
                dve.wait_ge(w_high, i + 1)
                nc.vector.tensor_tensor(wgt_half[1][:, s, :], w, wgt_half[0][:, s, :].bitcast(F32), ALU.subtract)\
                    .then_inc(w_ready, 1)

            def accumulate(g, outs=range(8)):
                for o in outs:
                    dve.wait_ge(up_done, g * 8 + (o + 1))
                    xs = x[:, o // 2, (o % 2) * 512:(o % 2 + 1) * 512]
                    nc.vector.tensor_tensor(xs, xs, psum[:, o % 4, :], ALU.add).then_inc(x_added, 1)

            dve.wait_ge(gate_done, SEQ // TB)
            for i in range(4):
                weigh(i, i, 16, True)
            accumulate(0)
            with dve.Fori(1, EARLY // 4) as r:
                for q in range(2):
                    for s in (2 * q, 2 * q + 1):
                        weigh(r * 4 + s, s, r * 16 + 16, True)
                    accumulate(r * 2 + (q - 1))
            for i in (EARLY, EARLY + 1):
                weigh(i, i % 4, 4 * EARLY + 16, False)
            accumulate(FIRST_D)
            with dve.Fori(EARLY // 4, NK // 4 - 1) as r:
                for s in (2, 3):
                    weigh(r * 4 + s, s, r * 16 + 16, False)
                accumulate(r * 2)
                for s in (0, 1):
                    weigh(r * 4 + (s + 4), s, r * 16 + 32, False)
                accumulate(r * 2 + 1)
            for i in (NK - 2, NK - 1):
                weigh(i, i % 4, 4 * NK, False)
            accumulate(GROUPS - 2)
            def final(t):
                dve.wait_ge(fin_sq, t + 1)
                nc.vector.tensor_scalar(ms[:, t:t + 1], ss[:, t:t + 1], 1.0 / D, EPS, ALU.mult, ALU.add)\
                    .then_inc(fin_mean, 1)
                dve.wait_ge(fin_root, t + 1)
                step(nc.vector.reciprocal(rs[:, t:t + 1], rt[:, t:t + 1]))
                nc.vector.scalar_tensor_tensor(hn[:, t, :], x[:, t, :], rs[:, t:t + 1], fin_w, ALU.mult, ALU.mult)\
                    .then_inc(fin_y, 1)

            dve.wait_ge(ld_fin, 16)
            for t in range(NT):
                accumulate(GROUPS - 1, (2 * t, 2 * t + 1))
                if t:
                    final(t - 1)
            dve.wait_ge(x_added, 8 * GROUPS + 4)
            final(NT - 1)

        @block.tensor
        def _(pe):
            pe.wait_ge(consts, 5)

            def turn(u):
                pe.wait_ge(u.h, 2 * u.tiles)
                for k in range(KC):
                    if k >= 4:
                        pe.wait_ge(u.ready, k - 3)
                    for t in range(u.tiles):
                        ins = nc.tensor.transpose(psum[:, 4 + k % 4, t * P:(t + 1) * P], u.dst[:, t, k * P:(k + 1) * P], ident)
                    ins.then_inc(u.tr, 1)

            def three(out, lhs, rhs, first, last):
                nc.tensor.matmul(out, lhs[0], rhs[0], start=first, stop=False)
                nc.tensor.matmul(out, lhs[0], rhs[1], start=False, stop=False)
                return nc.tensor.matmul(out, lhs[1], rhs[0], start=False, stop=last)

            def columns(b, s, rhs, n, bank):
                pe.wait_ge(low_ready, b + 1)
                for k in range(KC):
                    ins = three(psum[:, bank, 0:n], [w[:, s % 2, k * P:(k + 1) * P] for w in w_half],
                                [r[:, k, :] for r in rhs], k == 0, k == KC - 1)
                ins.then_inc(block_used, 1)

            def turned_columns(u, b, bank):
                pe.wait_ge(u.h, u.tiles)

                def turn_chunk(k):
                    for t in range(u.tiles):
                        ins = nc.tensor.transpose(psum[:, 4 + k % 4, t * P:(t + 1) * P], u.dst[:, t, k * P:(k + 1) * P], ident)
                    ins.then_inc(u.tr, 1)

                for k in range(4):
                    turn_chunk(k)
                pe.wait_ge(low_ready, b + 1)
                for k in range(KC):
                    pe.wait_ge(u.ready, k + 1)
                    ins = three(psum[:, bank, 0:u.tiles * P], [w[:, b % 2, k * P:(k + 1) * P] for w in w_half],
                                [r[:, k, :] for r in u.hT], k == 0, k == KC - 1)
                    if k == KC - 1:
                        ins.then_inc(block_used, 1)
                    if k + 4 < KC:
                        pe.wait_ge(u.h, 2 * u.tiles)
                        turn_chunk(k + 4)

            def rows(b, lhs, banks, k0, tile_done=None):
                pe.wait_ge(low_ready, b + 1)
                steps = [(j, n) for j in range(2) for n in range(len(banks))]
                if tile_done is not None:
                    steps = [(j, n) for n in range(len(banks)) for j in range(2)]
                for j, n in steps:
                    ins = three(psum[:, banks[n], :], [a[:, k0 + j, n * P:(n + 1) * P] for a in lhs],
                                [w[:, b % 2, j * 512:(j + 1) * 512] for w in w_half],
                                k0 + j == 0, k0 + j == KC - 1)
                    if tile_done is not None and j == 1 and n < len(banks) - 1:
                        ins.then_inc(tile_done, 1)
                ins.then_inc(block_used, 1)

            def transposed_keys():
                for h in range(HH):
                    pe.wait_ge(bank_free, 25 + h)
                    for t in range(NT):
                        ins = nc.tensor.transpose(psum[:, h, t * P:(t + 1) * P], G[:, h, t * P:(t + 1) * P], ident)
                    ins.then_inc(ke_tr, 1)

            turned_columns(mixn, 0, 0)
            for s in range(1, 4):
                columns(s, s, hT_half, SEQ, s)
            with pe.Fori(1, 3) as r:
                for s in range(4):
                    pe.wait_ge(bank_free, r * 4 + (s + 1))
                    columns(r * 4 + s, s, hT_half, SEQ, s)
            for s in range(4):
                rows(12 + s, hT_half, range(4, 8), 2 * s)
            pe.wait_ge(block_used, 16)
            pe.sem_inc(i_done, 1)
            for b in range(12):
                pe.wait_ge(bank_free, 12 + b + 1)
                columns(16 + b, b % 4, hT_half, SEQ, b % 4)
                if b == 1:
                    pe.wait_ge(i_out, NT)
                    turn(memn)
            pe.wait_ge(memn.ready, KC)
            pe.wait_ge(qk_ready, 1)
            for h in range(HH):
                for t in range(NT):
                    ins = nc.tensor.matmul(psum[:, 4 + h, t * P:(t + 1) * P], expN[:, h, t * P:(t + 1) * P],
                                           pQ[:, h, t * P:(t + 1) * P], start=True, stop=True)
                ins.then_inc(a_done, 1)
            transposed_keys()
            for b in range(4):
                pe.wait_ge(ke_out, b + 1)
                columns(28 + b, b, memT_half, NM, b)
            pe.wait_ge(a_ready, 1)
            pe.wait_ge(conv_sq, CC)
            for c in range(CC):
                ins = nc.tensor.matmul(psum[:, 4, :], ones, csq[:, c, :], start=(c == 0), stop=(c == CC - 1))
            ins.then_inc(conv_sum, 1)

            def state_parts(h):
                if h >= 2:
                    pe.wait_ge(s_ready, (h - 1) * (NCH - 1))
                for n in range(NCH - 1):
                    lo = (n % 2) * CH
                    ins = nc.tensor.matmul(psum[:, 2 * (h % 2) + n % 2, (n // 2) * P:(n // 2 + 1) * P],
                                           keN[lo:lo + CH, h, (n // 2) * P:(n // 2 + 1) * P],
                                           iN[lo:lo + CH, n // 2, h * P:(h + 1) * P], start=True, stop=True)
                ins.then_inc(u_done, 1)

            def values(b0, bank):
                for s in range(4):
                    rows(b0 + s, memT_half, range(bank, bank + MT), 2 * s)
                pe.wait_ge(block_used, b0 + 4)
                pe.sem_inc(v_done, 1)

            pe.wait_ge(k_out, 4)
            state_parts(0)
            state_parts(1)
            pe.wait_ge(a_ready, HH)
            values(32, 6)
            state_parts(2)
            state_parts(3)
            pe.wait_ge(conv_root, 1)
            for b in (4, 5):
                columns(32 + b, b % 4, memT_half, NM, b)
            for h in range(HH):
                pe.wait_ge(s_ready, (h + 1) * (NCH - 1))
                if h < 2:
                    pe.wait_ge(k_out, h + 5)
                else:
                    pe.wait_ge(v_out, h - 1)
                for t in range(NT):
                    nc.tensor.matmul(psum[:, 4 + h, t * P:(t + 1) * P], iN[:, t, h * P:(h + 1) * P],
                                     aT[:, h, t * P:(t + 1) * P], start=True, stop=False, skip_group_check=True)
                    for n in (2 * t, 2 * t + 1):
                        if n == 0:
                            continue
                        ins = nc.tensor.matmul(psum[:, 4 + h, n * CH:(n + 1) * CH], S[:, h, n, :],
                                               pQ[:, h, n * CH:(n + 1) * CH], start=False, stop=(n % 2 == 1),
                                               skip_group_check=True)
                ins.then_inc(o_done, 1)
            for h in range(HH):
                pe.wait_ge(o_sq, h + 1)
                if h >= 2:
                    pe.wait_ge(o_root, h - 1)
                nc.tensor.matmul(psum[:, 2 + h % 2, :], ones, sq[:, h, :], start=True, stop=True).then_inc(o_sum, 1)
                if h % 2:
                    columns(38 + h // 2, 2 + h // 2, memT_half, NM, h // 2)

            def product(lhs, b0, done, first, parts=None):
                for hf in range(2):
                    pe.wait_ge(*first[hf])
                    for s in range(4):
                        if parts is not None:
                            pe.wait_ge(parts, 2 * s + 2)
                        rows(b0 + 4 * hf + s, lhs, range(4 * hf, 4 * hf + 4), 2 * s,
                             done if hf and s == 3 else None)
                    pe.wait_ge(block_used, b0 + 4 * hf + 4)
                    pe.sem_inc(done, 1)

            pe.wait_ge(k_out, KC)
            product(hT_half, 40, mix_done, ((o_root, HH), (y_ready, KC)), y_ready)
            pe.wait_ge(x_mixed, NT)
            values(48, 2)
            for b in range(KC):
                if b >= 4:
                    pe.wait_ge(q_out, b - 3)
                if b == 0:
                    turned_columns(attn, 52, 0)
                else:
                    if b == 2:
                        pe.wait_ge(v_out, 2 * MT)
                    columns(52 + b, b, hT_half, SEQ, b % 4)

            def scores(h):
                if h >= 2:
                    pe.wait_ge(sc_exp, NT * (h - 1))
                for t in range(NT):
                    for c in range(2):
                        ins = nc.tensor.matmul(psum[:, 2 * (h % 2) + t // 2, (t % 2) * NM:(t % 2 + 1) * NM],
                                               qT[:, 2 * h + c, t * P:(t + 1) * P], KT[:, 2 * h + c, :],
                                               start=(c == 0), stop=(c == 1), skip_group_check=True)
                ins.then_inc(sc_done, 1)

            pe.wait_ge(q_out, KC - 2)
            scores(0)
            pe.wait_ge(q_out, KC)
            scores(1)
            for h in range(MH):
                pe.wait_ge(p_ready, NT * (h + 1))
                for m in range(MT):
                    if h:
                        pe.wait_ge(pT_out, MT * (h - 1) + m + 1)
                    for t in range(NT):
                        ins = nc.tensor.transpose(psum[:, 4 + m, t * P:(t + 1) * P], prob[:, h % 2, t, m * P:(m + 1) * P], ident)
                    ins.then_inc(p_tr, 1)
                if h + 2 < MH:
                    scores(h + 2)
                pe.wait_ge(pT_out, MT * (h + 1))
                for c in range(2):
                    if h:
                        pe.wait_ge(ao_out, 2 * (h - 1) + c + 1)
                    for m in range(MT):
                        ins = nc.tensor.matmul(psum[:, 6 + c, :], Vm[:, m, h * DH + c * P:h * DH + (c + 1) * P],
                                               pT[:, h % 2, m, :], start=(m == 0), stop=(m == MT - 1))
                    ins.then_inc(ao_done, 1)
            product(hT_half, 60, att_done, ((sc_exp, NT * MH), (ao_out, 2 * MH)), ao_out)
            turned_columns(ffnn, 68, 0)
            for s in range(1, 4):
                columns(68 + s, s, hT_half, SEQ, s)
            with pe.Fori(1, 4) as r:
                for s in range(4):
                    pe.wait_ge(qp_out, r * 4 + (s - 3))
                    columns(r * 4 + (68 + s), s, hT_half, SEQ, s)
            pe.wait_ge(ld_keys, 16)
            for b in range(16):
                if b < 4:
                    pe.wait_ge(qp_out, 4 * b + 4)
                if b >= 4:
                    pe.wait_ge(pk_out, b - 3)
                for j in range(4):
                    hp = 4 * (b % 4) + j
                    ins = nc.tensor.matmul(psum[:, 4 + b % 4, j * NK:(j + 1) * NK], qpT[:, hp, (b // 4) * P:(b // 4 + 1) * P],
                                           keysT[:, hp, :], start=True, stop=True)
                ins.then_inc(pk_done, 1)

            def first_product(i, s):
                pe.wait_ge(gelu_out, i + 1)
                columns(i + FRONT, s, hT_half, SEQ, 4 + s % 2)

            def gate_step(n, h):
                s = h % 2
                pe.wait_ge(hot_ready, n + 1)
                pe.wait_ge(gate_out, n + 1)
                for j in range(TB):
                    ins = nc.tensor.matmul(psum[:, 2 * s + j // 4, (j % 4) * P:(j % 4 + 1) * P],
                                           hot[:, h, 1, j * P:(j + 1) * P], hot[:, h, 0, j * P:(j + 1) * P],
                                           start=True, stop=True)
                ins.then_inc(gate_done, 1)

            def second_product(g, s):
                pe.wait_ge(up_low, g * GT + GT)
                pe.wait_ge(w_ready, g * GT + GT)
                for o in range(8):
                    pe.wait_ge(x_added, g * 8 + (o + 1))
                    for t in range(GT):
                        ins = three(psum[:, o % 4, :], [w[:, s + t, (o // 2) * P:(o // 2 + 1) * P] for w in wgt_half],
                                    [u[:, s + t, (o % 2) * 512:(o % 2 + 1) * 512] for u in up_half],
                                    t == 0, t == GT - 1)
                    ins.then_inc(up_done, 1)

            pe.wait_ge(pk_out, 14)
            for t in range(NT):
                with pe.Fori(TURN_AT[t - 1] // 4 if t else 0, TURN_AT[t] // 4) as r:
                    for s in range(4):
                        first_product(r * 4 + s, s)
                pe.wait_ge(hk_ready, t + 1)
                if t:
                    pe.wait_ge(hkT_out, t)
                for j in range(3):
                    ins = nc.tensor.transpose(psum[:, 6, j * P:(j + 1) * P], hk[:, j, :], ident)
                ins.then_inc(hk_tr, 1)
            with pe.Fori(0, SEQ // TB // HOTS // 4) as r:
                for g in range(4):
                    first_product(r * 4 + (AHEAD + g), g)
                    for h in range(HOTS):
                        gate_step(r * (4 * HOTS) + (g * HOTS + h), h)
            for i in range(DURING, EARLY):
                first_product(i, i % 4)
            pe.wait_ge(gate_out, SEQ // TB + 2)
            second_product(0, 0)
            with pe.Fori(0, (FIRST_D - 1) // 2) as r:
                second_product(r * 2 + 1, 2)
                second_product(r * 2 + 2, 0)
            first_product(EARLY, 0)
            first_product(EARLY + 1, 1)
            second_product(FIRST_D, 2)
            with pe.Fori(EARLY // 4, NK // 4 - 1) as r:
                first_product(r * 4 + 2, 2)
                first_product(r * 4 + 3, 3)
                second_product(r * 2, 0)
                first_product(r * 4 + 4, 0)
                first_product(r * 4 + 5, 1)
                second_product(r * 2 + 1, 2)
            first_product(NK - 2, 2)
            first_product(NK - 1, 3)
            second_product(GROUPS - 2, 0)
            second_product(GROUPS - 1, 2)


def kernel(**inputs):
    import numpy as np
    import concourse.bacc as bacc
    from concourse.bass_utils import run_bass_kernel_spmd

    def cols(w):
        return w.reshape(KC, P, -1, P).transpose(2, 1, 0, 3).reshape(-1, P, D)

    def rws(w):
        return w.reshape(4, 2, P, -1, 512).transpose(3, 0, 2, 1, 4).reshape(-1, P, D)

    def vec(v):
        return v.reshape(-1, P).T

    i = {k: np.asarray(v) for k, v in inputs.items()}
    w_in, wkv = i["w_in"][0], i["wkv_mem"][0]
    o0 = 3 * CW
    front = np.ascontiguousarray(np.concatenate([
        cols(w_in[:, o0:o0 + 2 * CW]), cols(w_in[:, o0 + 3 * CW:]), rws(w_in[:, o0 + 2 * CW:o0 + 3 * CW]),
        cols(w_in[:, :o0]),
        cols(wkv[:, :D // 2]), rws(wkv[:, D:D + D // 2]), cols(wkv[:, D // 2:D]), rws(i["w_out"][0]),
        rws(wkv[:, D + D // 2:]), cols(i["wq_mem"][0]), rws(i["wo_mem"][0]),
        cols(i["peer_w_query"][0])]))
    vecs = np.ascontiguousarray(np.concatenate([
        vec(i["mix_norm_w"][0]), vec(i["conv_norm_w"][0]), vec(i["hgrn_norm_w"][0]), vec(i["hgrn_lb_logits"][0]),
        vec(i["hgrn_lb_logits"][1]), vec(i["xattn_norm_w"][0]), vec(i["mem_norm_w"][0]), vec(i["ffn_norm_w"][0]),
        vec(i["conv_w"][0].reshape(-1))], axis=1))
    down = i["peer_down"][0].reshape(NK, P, KC, P).transpose(0, 3, 2, 1).reshape(NK, P, D)
    arrays = {
        "x_in": i["x"][0], "mem_in": i["mem"][0], "vecs_in": vecs, "final_in": i["final_norm_w"].reshape(1, D),
        "front_w": front, "keys_in": i["peer_sub_keys"][0].reshape(16, NK, P).transpose(2, 0, 1),
        "down_in": down, "up_in": i["peer_up"][0].reshape(NK, P, D)}
    arrays = {k: np.ascontiguousarray(v) for k, v in arrays.items()}
    nc = bacc.Bacc("TRN2", target_bir_lowering=False, num_devices=1)
    args = [nc.dram_tensor(k, v.shape, mybir.dt.from_np(v.dtype), kind="ExternalInput").ap() for k, v in arrays.items()]
    args.append(nc.dram_tensor("out", (SEQ, D), F32, kind="ExternalOutput").ap())
    args.append(nc.dram_tensor("gate_dram", (P, NCH, NK * CH), F32, kind="Internal").ap())
    args.append(nc.dram_tensor("hid_dram", (EARLY, P, SEQ), F32, kind="Internal").ap())
    build(nc, *args)
    r = run_bass_kernel_spmd(nc, [arrays], core_ids=[0])
    return r.results[0]["out"].reshape(1, SEQ, D)
```
